# Optimizing a Trainium2 kernel written in Bass

```python
import jax
import jax.numpy as jnp
from jax import lax
import numpy as np

D_MODEL = 1024
BATCH = 1
SEQ = 512
DEPTH = 1

HEAD_DIM = 64
MIX_WIDTH = D_MODEL
FOX_WIDTH = MIX_WIDTH // 2
NSA_WIDTH = MIX_WIDTH - FOX_WIDTH
FOX_HEADS = FOX_WIDTH // HEAD_DIM
NSA_HEADS = NSA_WIDTH // HEAD_DIM
NSA_KV_HEADS = 2
NSA_GROUP = NSA_HEADS // NSA_KV_HEADS
NSA_KV_WIDTH = NSA_KV_HEADS * HEAD_DIM
Q_BLOCK = 128
CMP_BLOCK = 32
CMP_STRIDE = 16
CMP_HIDDEN = 2 * HEAD_DIM
SLC_BLOCK = 64
N_SELECT = 16
WINDOW = 512
ROPE_THETA = 10000.0
RMS_EPS = 1e-6
SLC_RATIO = SLC_BLOCK // CMP_STRIDE
CMP_PAD_LEFT = CMP_BLOCK // CMP_STRIDE - 1
N_OVERLAP = (SLC_BLOCK + CMP_BLOCK) // CMP_STRIDE - 1
IN_SPLITS = (FOX_WIDTH, FOX_WIDTH, FOX_WIDTH, FOX_HEADS, FOX_WIDTH,
             NSA_WIDTH, NSA_KV_WIDTH, NSA_KV_WIDTH, NSA_KV_WIDTH, NSA_KV_WIDTH,
             NSA_KV_WIDTH, NSA_KV_WIDTH, 3 * NSA_HEADS, NSA_WIDTH)
IN_WIDTH = 4 * FOX_WIDTH + FOX_HEADS + 2 * NSA_WIDTH + 6 * NSA_KV_WIDTH + 3 * NSA_HEADS

kernel_name = 'hybrid_fox_nsa_block'

def rms_norm(x, g):
    xf = x.astype(jnp.float32)
    y = xf * lax.rsqrt(jnp.mean(xf * xf, axis=-1, keepdims=True) + RMS_EPS)
    return y.astype(x.dtype) * g

def rope_tables(seq_len):
    inv = 1.0 / (ROPE_THETA ** (jnp.arange(0, HEAD_DIM, 2, dtype=jnp.float32) / HEAD_DIM))
    ang = jnp.arange(seq_len, dtype=jnp.float32)[:, None] * inv[None, :]
    return jnp.cos(ang), jnp.sin(ang)

def apply_rope(t, cos, sin):
    t1, t2 = jnp.split(t.astype(jnp.float32), 2, axis=-1)
    out = jnp.concatenate([t1 * cos - t2 * sin, t2 * cos + t1 * sin], axis=-1)
    return out.astype(t.dtype)

def masked_softmax(logits, mask):
    logits = jnp.where(mask, logits.astype(jnp.float32), -jnp.inf)
    m = jnp.max(logits, axis=-1, keepdims=True)
    m = jnp.where(jnp.isfinite(m), m, 0.0)
    p = jnp.exp(logits - m)
    return p / jnp.maximum(jnp.sum(p, axis=-1, keepdims=True), 1e-30)

def fox_attention(q, k, v, log_f):
    b, h, s, d = q.shape
    scale = d ** -0.5
    cum = jnp.cumsum(log_f.astype(jnp.float32), axis=-1)
    kpos = jnp.arange(s)

    def block(i):
        q0 = i * Q_BLOCK
        qb = lax.dynamic_slice_in_dim(q, q0, Q_BLOCK, axis=2)
        cb = lax.dynamic_slice_in_dim(cum, q0, Q_BLOCK, axis=2)
        tq = q0 + jnp.arange(Q_BLOCK)
        logits = (jnp.einsum('bhqd,bhkd->bhqk', qb, k, preferred_element_type=jnp.float32) * scale
                  + cb[..., :, None] - cum[..., None, :])
        p = masked_softmax(logits, kpos[None, :] <= tq[:, None])
        return jnp.einsum('bhqk,bhkd->bhqd', p.astype(v.dtype), v)

    o = lax.map(block, jnp.arange(s // Q_BLOCK))
    return o.transpose(1, 2, 0, 3, 4).reshape(b, h, s, d)

def nsa_compress(t, w1, w2, pe):
    b, g, s, d = t.shape
    n_cmp = (s - CMP_BLOCK) // CMP_STRIDE + 1
    idx = jnp.arange(n_cmp)[:, None] * CMP_STRIDE + jnp.arange(CMP_BLOCK)[None, :]
    blocks = (t[:, :, idx, :] + pe).reshape(b, g, n_cmp, CMP_BLOCK * d)
    return jax.nn.silu(blocks @ w1) @ w2

def nsa_attention(q, kc, vc, ks, vs, kw, vw, gates):
    b, g, hg, s, d = q.shape
    scale = d ** -0.5
    n_cmp = kc.shape[2]
    n_blk = s // SLC_BLOCK
    n_sel = min(N_SELECT, n_blk)
    cmp_end = jnp.arange(n_cmp) * CMP_STRIDE + CMP_BLOCK - 1
    sel_idx = jnp.arange(n_blk)[:, None] * SLC_RATIO + jnp.arange(N_OVERLAP)[None, :]
    pad_right = max(0, (n_blk - 1) * SLC_RATIO + N_OVERLAP - n_cmp - CMP_PAD_LEFT)
    ks_blk = ks.reshape(b, g, n_blk, SLC_BLOCK, d)
    vs_blk = vs.reshape(b, g, n_blk, SLC_BLOCK, d)
    kw_pad = jnp.pad(kw, ((0, 0), (0, 0), (WINDOW, 0), (0, 0)))
    vw_pad = jnp.pad(vw, ((0, 0), (0, 0), (WINDOW, 0), (0, 0)))
    bi = jnp.arange(b)[:, None, None, None]
    gi = jnp.arange(g)[None, :, None, None]
    blk = jnp.arange(n_blk)

    def block(i):
        q0 = i * Q_BLOCK
        tq = q0 + jnp.arange(Q_BLOCK)
        qb = lax.dynamic_slice_in_dim(q, q0, Q_BLOCK, axis=3)
        gb = lax.dynamic_slice_in_dim(gates, q0, Q_BLOCK, axis=3)
        lc = jnp.einsum('bghqd,bgkd->bghqk', qb, kc, preferred_element_type=jnp.float32) * scale
        pc = masked_softmax(lc, cmp_end[None, :] <= tq[:, None])
        oc = jnp.einsum('bghqk,bgkd->bghqd', pc.astype(vc.dtype), vc)
        imp = jnp.pad(pc.sum(axis=2), ((0, 0), (0, 0), (0, 0), (CMP_PAD_LEFT, pad_right)))
        imp = imp[..., sel_idx].sum(axis=-1)
        cur = (tq // SLC_BLOCK)[:, None]
        forced = (blk[None, :] == 0) | (blk[None, :] == cur) | (blk[None, :] == cur - 1)
        imp = jnp.where(forced, jnp.inf, jnp.where(blk[None, :] > cur, -jnp.inf, imp))
        _, top = lax.top_k(imp, n_sel)
        k_sel = ks_blk[bi, gi, top].reshape(b, g, Q_BLOCK, n_sel * SLC_BLOCK, d)
        v_sel = vs_blk[bi, gi, top].reshape(b, g, Q_BLOCK, n_sel * SLC_BLOCK, d)
        sel_pos = (top[..., None] * SLC_BLOCK + jnp.arange(SLC_BLOCK)).reshape(b, g, Q_BLOCK, n_sel * SLC_BLOCK)
        ls = jnp.einsum('bghqd,bgqkd->bghqk', qb, k_sel, preferred_element_type=jnp.float32) * scale
        ps = masked_softmax(ls, (sel_pos <= tq[:, None])[:, :, None])
        o_sel = jnp.einsum('bghqk,bgqkd->bghqd', ps.astype(v_sel.dtype), v_sel)
        kwb = lax.dynamic_slice_in_dim(kw_pad, q0, WINDOW + Q_BLOCK, axis=2)
        vwb = lax.dynamic_slice_in_dim(vw_pad, q0, WINDOW + Q_BLOCK, axis=2)
        wpos = q0 - WINDOW + jnp.arange(WINDOW + Q_BLOCK)
        dist = tq[:, None] - wpos[None, :]
        wmask = (dist >= 0) & (dist < WINDOW) & (wpos[None, :] >= 0)
        lw = jnp.einsum('bghqd,bgkd->bghqk', qb, kwb, preferred_element_type=jnp.float32) * scale
        pw = masked_softmax(lw, wmask)
        ow = jnp.einsum('bghqk,bgkd->bghqd', pw.astype(vwb.dtype), vwb)
        return gb[..., 0:1] * oc + gb[..., 1:2] * o_sel + gb[..., 2:3] * ow

    o = lax.map(block, jnp.arange(s // Q_BLOCK))
    return o.transpose(1, 2, 3, 0, 4, 5).reshape(b, g * hg, s, d)

def hybrid_layer(x, c, g_pre, g_post, w_ada, b_ada, w_in, b_forget, w_cmp_k1, w_cmp_k2,
                 w_cmp_v1, w_cmp_v2, pe_cmp_k, pe_cmp_v, w_out, cos, sin):
    b, s, _ = x.shape
    shift, scale, gate = jnp.split(jax.nn.silu(c) @ w_ada + b_ada, 3, axis=-1)
    h = rms_norm(x, g_pre) * (1.0 + scale[:, None, :]) + shift[:, None, :]
    proj = h @ w_in
    offsets = [int(o) for o in np.cumsum(IN_SPLITS)[:-1]]
    (fq, fk, fv, ff, fz, nq, kc, vc, ks, vs, kw, vw, ng, nz) = jnp.split(proj, offsets, axis=-1)

    def heads(t, n):
        return t.reshape(b, s, n, HEAD_DIM).transpose(0, 2, 1, 3)

    log_f = jax.nn.log_sigmoid((ff + b_forget).astype(jnp.float32)).transpose(0, 2, 1)
    o_fox = fox_attention(heads(fq, FOX_HEADS), heads(fk, FOX_HEADS), heads(fv, FOX_HEADS), log_f)
    y_fox = o_fox.transpose(0, 2, 1, 3).reshape(b, s, FOX_WIDTH) * jax.nn.silu(fz)

    q_n = apply_rope(heads(nq, NSA_HEADS), cos, sin).reshape(b, NSA_KV_HEADS, NSA_GROUP, s, HEAD_DIM)
    kc_c = nsa_compress(apply_rope(heads(kc, NSA_KV_HEADS), cos, sin), w_cmp_k1, w_cmp_k2, pe_cmp_k)
    vc_c = nsa_compress(heads(vc, NSA_KV_HEADS), w_cmp_v1, w_cmp_v2, pe_cmp_v)
    gates = jax.nn.sigmoid(ng).reshape(b, s, NSA_HEADS, 3).transpose(0, 2, 1, 3)
    gates = gates.reshape(b, NSA_KV_HEADS, NSA_GROUP, s, 3)
    o_nsa = nsa_attention(q_n, kc_c, vc_c,
                          apply_rope(heads(ks, NSA_KV_HEADS), cos, sin), heads(vs, NSA_KV_HEADS),
                          apply_rope(heads(kw, NSA_KV_HEADS), cos, sin), heads(vw, NSA_KV_HEADS),
                          gates)
    y_nsa = o_nsa.transpose(0, 2, 1, 3).reshape(b, s, NSA_WIDTH) * jax.nn.silu(nz)

    y = jnp.concatenate([y_fox, y_nsa], axis=-1) @ w_out
    return x + gate[:, None, :] * rms_norm(y, g_post)

def setup_inputs(seed: int = 0) -> dict:
    key = jax.random.key(seed)
    ks = jax.random.split(key, 16)
    f32 = jnp.float32

    def nrm(k, shape, fan_in):
        return jax.random.normal(k, shape, f32) * (fan_in ** -0.5)

    flat = CMP_BLOCK * HEAD_DIM
    return {
        'x': jax.random.normal(ks[0], (BATCH, SEQ, D_MODEL), f32),
        'c': jax.random.normal(ks[1], (BATCH, D_MODEL), f32),
        'g_pre': 1.0 + 0.05 * jax.random.normal(ks[2], (DEPTH, D_MODEL), f32),
        'g_post': 1.0 + 0.05 * jax.random.normal(ks[3], (DEPTH, D_MODEL), f32),
        'w_ada': nrm(ks[4], (DEPTH, D_MODEL, 3 * D_MODEL), D_MODEL),
        'b_ada': 0.01 * jax.random.normal(ks[5], (DEPTH, 3 * D_MODEL), f32),
        'w_in': nrm(ks[6], (DEPTH, D_MODEL, IN_WIDTH), D_MODEL),
        'b_forget': jax.random.uniform(ks[7], (DEPTH, FOX_HEADS), f32, 3.0, 6.0),
        'w_cmp_k1': nrm(ks[8], (DEPTH, flat, CMP_HIDDEN), flat),
        'w_cmp_k2': nrm(ks[9], (DEPTH, CMP_HIDDEN, HEAD_DIM), CMP_HIDDEN),
        'w_cmp_v1': nrm(ks[10], (DEPTH, flat, CMP_HIDDEN), flat),
        'w_cmp_v2': nrm(ks[11], (DEPTH, CMP_HIDDEN, HEAD_DIM), CMP_HIDDEN),
        'pe_cmp_k': 0.1 * jax.random.normal(ks[12], (DEPTH, CMP_BLOCK, HEAD_DIM), f32),
        'pe_cmp_v': 0.1 * jax.random.normal(ks[13], (DEPTH, CMP_BLOCK, HEAD_DIM), f32),
        'w_out': nrm(ks[14], (DEPTH, MIX_WIDTH, D_MODEL), MIX_WIDTH),
    }

def reference(x, c, g_pre, g_post, w_ada, b_ada, w_in, b_forget, w_cmp_k1, w_cmp_k2,
              w_cmp_v1, w_cmp_v2, pe_cmp_k, pe_cmp_v, w_out):
    cos, sin = rope_tables(x.shape[1])
    for layer in range(DEPTH):
        x = hybrid_layer(x, c, g_pre[layer], g_post[layer], w_ada[layer], b_ada[layer],
                         w_in[layer], b_forget[layer], w_cmp_k1[layer], w_cmp_k2[layer],
                         w_cmp_v1[layer], w_cmp_v2[layer], pe_cmp_k[layer], pe_cmp_v[layer],
                         w_out[layer], cos, sin)
    return x


_drawn_inputs = setup_inputs


def setup_inputs(seed=0):
    import zlib

    import numpy as np

    out = dict(_drawn_inputs(seed))
    spreads = {}
    factors = {'b_ada': 4.216, 'pe_cmp_k': 8.0, 'pe_cmp_v': 3.267}
    for name, (base, spread) in spreads.items():
        noise = np.random.default_rng([zlib.crc32(name.encode()), seed]).standard_normal(out[name].shape)
        drawn = base * np.exp(spread * noise) if base else spread * noise
        out[name] = jnp.asarray(drawn.astype(out[name].dtype))
    for name, factor in factors.items():
        out[name] = (out[name] * factor).astype(out[name].dtype)
    return out
```

```python
from contextlib import ExitStack

import concourse.bass as bass
from concourse import mybir

F32 = mybir.dt.float32
R32 = mybir.dt.float32r
ALU = mybir.AluOpType
ACT = mybir.ActivationFunctionType
AX_X = mybir.AxisListType.X

P = 128
SEQ = 512
DM = 1024
HD = 64
NT = SEQ // P
KD = DM // P
FOX_W = DM // 2
FOX_H = FOX_W // HD
NSA_H = FOX_H
KV_W = 2 * HD
CMP_BLOCK, CMP_STRIDE = 32, 16
NCMP = (SEQ - CMP_BLOCK) // CMP_STRIDE + 1
NC = NCMP + 1
KC = CMP_BLOCK * HD // P
EPS = 1e-6
NEG = -1.0e30
QSCALE = HD ** -0.5

C_FQ, C_FK, C_FV, C_FF = 0, FOX_W, 2 * FOX_W, 3 * FOX_W
C_FZ = C_FF + FOX_H
C_NQ = C_FZ + FOX_W
C_KC = C_NQ + FOX_W
C_VC, C_KS, C_VS, C_KW, C_VW = (C_KC + i * KV_W for i in range(1, 6))
C_NG = C_KC + 6 * KV_W
C_NZ = C_NG + 3 * NSA_H

R_C, R_GPRE, R_ADA, R_GPOST, R_PEK, R_PEV, R_END = 0, 8, 16, 40, 48, 64, 80

K_ID, K_MASK, K_CMASK, K_SEL, K_END = 0, 128, 256, 256 + NT * NC, 256 + NT * NC + 8

PROLOGUE = [("vecsT", 0), ("ada", 0)] + [("xT", d) for d in range(KD)] + [
    ("vsw", 0), ("vsw", 1), ("ffng", 0), ("kc", 0), ("ffT", 0),
    ("fv", 0), ("fv", 1), ("fv", 2), ("fv", 3), ("fq", 0), ("fk", 0)]
FILL = [
    [("fq", 1), ("fk", 1)], [("fz", 0), ("vc", 0)], [("fq", 2), ("fk", 2)], [("fz", 1), ("hidk", 0)],
    [("fq", 3), ("fk", 3)], [("fz", 2), ("kc2", 0), ("ks", 0)], [("nq", 0), ("hidv", 0)],
    [("fz", 3), ("kw", 0), ("vc2", 0)],
    [("Sc", 0)], [("PcT", 0)], [("nz", 0)], [("nq", 1)],
    [("Sc", 1), ("gate", 0)], [("PcT", 1), ("gate", 1)], [("nz", 1)], [("nq", 2)],
    [("Sc", 2), ("gate", 2)], [("PcT", 2), ("gate", 3)], [("nz", 2)], [("nq", 3)],
    [("Sc", 3), ("gate", 4)], [("PcT", 3), ("gate", 5)], [("nz", 3)], [("gate", 6), ("gate", 7)],
]
JOBS = PROLOGUE + [j for f in FILL for j in f]
JOB = {j: n for n, j in enumerate(JOBS)}
READERS = dict(vecsT="D", ada="D", xT="AD", vsw="AD", ffng="AD", kc="AD", ffT="D", fv="AD", fq="AD",
               fk="AD", fz="AD", vc="A", hidk="AD", hidv="AD", kc2="AD", vc2="A", ks="AD", nq="AD",
               kw="AD", nz="AD", Sc="D", PcT="A", gate="AD")


def emptied(who, n):
    return sum(who in READERS[k] for k, _ in JOBS[:n + 1])


def units_of(job):
    kind, i = job
    if kind == "ada":
        return [("ada", n) for n in range(16)]
    if kind == "vsw":
        return [("vs", 0), ("vw", 0)] if i == 0 else []
    if kind == "fv":
        return [("fv", i), ("fv", i + 1)] if i in (0, 2) else []
    if kind in ("hidk", "hidv"):
        return [(kind, 0), (kind, 1)]
    if kind in ("ffng", "kc", "fq", "fk", "fz", "vc", "ks", "nq", "kw", "nz", "gate"):
        return [job]
    return []


UNITS = [u for j in JOBS for u in units_of(j)] + [("wo", k) for k in range(KD)]
UNIT = {u: n for n, u in enumerate(UNITS)}
DIRECT = ("ada", "hidk", "hidv", "gate")
SPLIT = [u for u in UNITS if u[0] not in DIRECT]
SPLITN = {u: n for n, u in enumerate(SPLIT)}
ROPED = [j for j in JOBS if j[0] in ("kc", "ks", "kw", "nq")]
ROPEN = {j: n for n, j in enumerate(ROPED)}
NRAW, NSPLIT = 4, 4
TWO = ("ffng", "nq", "nz")


def dmas_of(u):
    return 2 if u[0] in TWO or (u[0] == "wo" and u[1] >= KD // 2) else 1


def landed(n):
    return 16 * sum(dmas_of(UNITS[m]) for m in range(n % NRAW, n + 1, NRAW))


JOB_OF = {u: JOB[j] for j in JOBS for u in units_of(j)}
JOB_OF["fv", 0], JOB_OF["fv", 1] = JOB["fv", 1], JOB["fv", 1]
JOB_OF["fv", 2], JOB_OF["fv", 3] = JOB["fv", 3], JOB["fv", 3]
JOB_OF["vs", 0], JOB_OF["vw", 0] = JOB["vsw", 1], JOB["vsw", 1]
MIDJOB = [("ada", n) for n in range(15)] + [("hidk", 0), ("hidv", 0)]


INST = [(p, a, None) for p in range(4) for a in range(2)]
INST += [(4 + t, a, b) for t in range(4) for a in range(2) for b in range(2)]
NI = len(INST)
LAST_OF_PAIR = [max(s for s, i in enumerate(INST) if i[0] == p) for p in range(8)]
QT = [(3, 0, 0, 512), (2, 1, 0, 384), (0, 1, 384, 128), (1, 2, 0, 256)]
POFF = {q: g * 512 + c for q, g, c, _ in QT}
PTG = [[(0, 0)], [(1, 0), (3, 384)], [(2, 0)]]
PTW = [512, 512, 256]


def head_of(s):
    p, a, _ = INST[s]
    return 2 * p + a


def first_of_head(s):
    return INST[s][2] in (None, 0)


def last_of_head(s):
    return INST[s][2] in (None, 1)


def hybrid_layer_kernel(nc, x, c, g_pre, g_post, w_ada, b_ada, w_in, b_forget, w_cmp_k1, w_cmp_k2,
                        w_cmp_v1, w_cmp_v2, pe_cmp_k, pe_cmp_v, w_out, rope, consts, out):
    with ExitStack() as ctx:
        def sb(name, shape, dt=F32, scope=None):
            return (scope or ctx).enter_context(nc.sbuf_tensor(name, shape, dt))

        def sem(name):
            return ctx.enter_context(nc.semaphore(name))

        bank = [ctx.enter_context(nc.psum_tensor(f"bank{i}", [P, 512], F32)) for i in range(8)]
        S_BANK, PT_BANK, Y_BANK, PJ_BANK = bank[0:3], bank[3:5], bank[5], bank[6:8]

        hT_hi = sb("hT_hi", [P, KD, SEQ], R32)
        hT_lo = sb("hT_lo", [P, KD, SEQ], R32)
        raw = sb("raw", [P, NRAW, KD, P])
        w_hi = sb("w_hi", [P, NSPLIT, KD, P], R32)
        w_lo = sb("w_lo", [P, NSPLIT, KD, P], R32)
        nk_hi = sb("nk_hi", [P, 2, SEQ], R32)
        nk_lo = sb("nk_lo", [P, 2, SEQ], R32)
        cs = sb("cs", [P, 2, SEQ])
        t_sb = sb("t_sb", [P, SEQ])
        t_swap = sb("t_swap", [P, SEQ])
        t_rope = sb("t_rope", [P, SEQ])
        vn_hi = sb("vn_hi", [P, NT, 2, P], R32)
        vn_lo = sb("vn_lo", [P, NT, 2, P], R32)
        prob = sb("prob", [P, 2, 1280])
        pt_hi = sb("pt_hi", [P, 3, 512], R32)
        pt_lo = sb("pt_lo", [P, 3, 512], R32)
        sz = sb("sz", [P, 2, SEQ])
        kon = sb("kon", [P, K_END])
        ident_r = sb("ident_r", [P, P], R32)
        mask_r = sb("mask_r", [P, P], R32)
        sel_r = sb("sel_r", [P, 8], R32)
        cum_r = sb("cum_r", [P, SEQ], R32)
        vecs = sb("vecs", [R_END, P])
        vecsT = sb("vecsT", [P, R_END])
        mod = sb("mod", [P, 16])
        amul = sb("amul", [P, KD])
        silc = sb("silc", [P, 2, KD])
        ssq = sb("ssq", [P, 8])
        rstd = sb("rstd", [P, 8])
        mhalf = sb("mhalf", [P, 4])
        ffc = sb("ffc", [P, NT, 8])
        bf = sb("bf", [8, 1])
        gates = sb("gates", [P, NT, 24])
        negm = sb("negm", [P, 2, 4])
        psum_row = sb("psum_row", [P, 2, 4])
        rinv = sb("rinv", [P, 2, 4])
        gg = sb("gg", [P, DM])
        w2k = sb("w2k", [P, 2, HD])
        w2v = sb("w2v", [P, HD])
        hid = sb("hid", [P, 2, NC])
        kcb_hi = sb("kcb_hi", [P, 2 * NC], R32)
        kcb_lo = sb("kcb_lo", [P, 2 * NC], R32)
        vcb = sb("vcb", [2 * NC, P])
        pc = sb("pc", [P, NT, 2, NC])
        pcs = sb("pcs", [P, 3, NT * 2])
        pcT = sb("pcT", [2 * NC, SEQ])
        with ExitStack() as early:
            x_sb = sb("x_sb", [P, NT, DM], F32, early)
        with ExitStack() as mid:
            qk_hi = sb("qk_hi", [P, 2, 2, SEQ], R32, mid)
            qk_lo = sb("qk_lo", [P, 2, 2, SEQ], R32, mid)
        with ExitStack() as late:
            x_res = sb("x_res", [P, NT, DM], F32, late)
        ctx.enter_context(nc.sbuf_tensor("hold", [P, NT, DM], F32))
        with ExitStack() as ffs:
            fz = sb("ff_z", [8, SEQ], F32, ffs)
            fe = sb("ff_e", [8, SEQ], F32, ffs)
            fc = sb("ff_c", [8, SEQ], F32, ffs)
            fo = sb("ff_o", [8, SEQ], F32, ffs)
        y32 = sb("y32", [P, KD, SEQ])
        vf_hi = sb("vf_hi", [P, NT, SEQ], R32)
        vf_lo = sb("vf_lo", [P, NT, SEQ], R32)
        U = sb("U", [P, 2, SEQ])
        B = sb("B", [P, KC, 2, NCMP])

        raw_landed = [sem(f"raw_landed{i}") for i in range(NRAW)]
        raw_used, split_done, wo_used = sem("raw_used"), sem("split_done"), sem("wo_used")
        x_in = [sem(f"x_in{i}") for i in range(NT)]
        xres_in, vecs_in, kon_in, rope_in, small_in = (sem(n) for n in (
            "xres_in", "vecs_in", "kon_in", "rope_in", "small_in"))
        sq_done, var_done, rstd_done, xn_done = (sem(n) for n in ("sq_done", "var_done", "rstd_done", "xn_done"))
        consts_done, fills_done = sem("consts_done"), sem("fills_done")
        tanhc_done, silc_done, mod_done = (sem(n) for n in ("tanhc_done", "silc_done", "mod_done"))
        pj_ready, pj_act, pj_dve = sem("pj_ready"), sem("pj_act"), sem("pj_dve")
        ff_abs, ff_ln, ff_cum, ff_hi, ff_lo, ff_e = (sem(n) for n in (
            "ff_abs", "ff_ln", "ff_cum", "ff_hi", "ff_lo", "ff_e"))
        gates_done = sem("gates_done")
        t_swapped, rope_done = sem("t_swapped"), sem("rope_done")
        u_moved, b_done, hid_done = sem("u_moved"), sem("b_done"), sem("hid_done")
        s_ready, max_done, exp_done, p_ready = (sem(n) for n in ("s_ready", "max_done", "exp_done", "p_ready"))
        pt_ready, pt_hi_done, pt_lo_done, pv_done = (sem(n) for n in ("pt_ready", "pt_hi_done", "pt_lo_done", "pv_done"))
        y_ready, y_done = sem("y_ready"), sem("y_done")
        c_shift, c_exp, c_prob = sem("c_shift"), sem("c_exp"), sem("c_prob")
        yh_done, yl_done = sem("yh_done"), sem("yl_done")
        o_ready, osq_done, ovar_done, orstd_done, o_done, stored = (sem(n) for n in (
            "o_ready", "osq_done", "ovar_done", "orstd_done", "o_done", "stored"))
        dve_own, pool_own = sem("dve_own"), sem("pool_own")

        ident = kon[:, K_ID:K_ID + P]
        block = ctx.enter_context(nc.Block())

        @block.sync
        def _(sp):
            w_in_k = w_in.rearrange("(k p) n -> p k n", p=P)
            w_ada_k = w_ada.rearrange("(k p) n -> p k n", p=P)
            first_col = dict(vs=C_VS, vw=C_VW, kc=C_KC, vc=C_VC, ks=C_KS, kw=C_KW)
            tile_col = dict(fv=C_FV, fq=C_FQ, fk=C_FK, fz=C_FZ)

            def pieces(kind, i, dst):
                if kind == "ada":
                    return [(dst, w_ada_k[:, :, i * P:(i + 1) * P])]
                if kind == "gate":
                    return [(dst, w_ada_k[:, :, 2 * DM + i * P:2 * DM + (i + 1) * P])]
                if kind in ("hidk", "hidv"):
                    w1 = (w_cmp_k1 if kind == "hidk" else w_cmp_v1).rearrange("(k p) n -> p k n", p=P)
                    return [(dst, w1[:, 8 * i:8 * i + 8, :])]
                if kind == "ffng":
                    return [(dst[:, :, 0:8], w_in_k[:, :, C_FF:C_FF + 8]),
                            (dst[:, :, 8:32], w_in_k[:, :, C_NG:C_NG + 24])]
                if kind in ("nq", "nz"):
                    c0 = (C_NQ if kind == "nq" else C_NZ) + i * HD
                    return [(dst[:, :, 0:HD], w_in_k[:, :, c0:c0 + HD]),
                            (dst[:, :, HD:P], w_in_k[:, :, c0 + 4 * HD:c0 + 5 * HD])]
                if kind == "wo":
                    if i < KD // 2:
                        return [(dst.rearrange("p k n -> p (k n)"), w_out[i * P:(i + 1) * P, :])]
                    r0 = FOX_W + (i - KD // 2) * HD
                    return [(dst[0:HD].rearrange("p k n -> p (k n)"), w_out[r0:r0 + HD, :]),
                            (dst[HD:P].rearrange("p k n -> p (k n)"), w_out[r0 + 4 * HD:r0 + 5 * HD, :])]
                c0 = first_col[kind] if kind in first_col else tile_col[kind] + i * P
                return [(dst, w_in_k[:, :, c0:c0 + P])]

            for n, (kind, i) in enumerate(UNITS):
                if n >= NRAW:
                    before = UNITS[n - NRAW]
                    if before in MIDJOB:
                        sp.wait_ge(raw_used, MIDJOB.index(before) + 1)
                    elif before[0] in DIRECT:
                        sp.wait_ge(pj_ready, JOB_OF[before] + 1)
                    else:
                        sp.wait_ge(split_done, SPLITN[before] + 1)
                for dst, src in pieces(kind, i, raw[:, n % NRAW, :, :]):
                    sp.dma_start(dst, src).then_inc(raw_landed[n % NRAW], 16)
            sp.wait_ge(s_ready, 3 * NI)
            for m in range(NT):
                sp.dma_start(x_res[:, m, :], x[m * P:(m + 1) * P, :]).then_inc(xres_in, 16)
            for m in range(NT):
                sp.wait_ge(o_done, 2 * (m + 1))
                sp.dma_start(out[m * P:(m + 1) * P, :], x_res[:, m, :]).then_inc(stored, 16)
            sp.wait_ge(stored, 16 * NT)

        @block.gpsimd
        def _(pool):
            own = [0]

            def link(ins):
                own[0] += 1
                ins.then_inc(pool_own, 1)
                pool.wait_ge(pool_own, own[0])

            pool.memset(mhalf[:, :], -0.5).then_inc(fills_done, 1)
            pool.memset(kcb_hi[:, :].bitcast(F32), 0.0).then_inc(fills_done, 1)
            pool.memset(kcb_lo[:, :].bitcast(F32), 0.0).then_inc(fills_done, 1)
            pool.memset(vcb[:, :], 0.0).then_inc(fills_done, 1)
            pool.memset(hid[:, :, :], 0.0).then_inc(fills_done, 1)
            pool.memset(cum_r[:, :].bitcast(F32), 0.0).then_inc(fills_done, 1)
            pool.memset(fo[:, :], 1.0).then_inc(fills_done, 1)
            pool.wait_ge(fills_done, 1)
            pool.wait_ge(var_done, 1)
            pool.tensor_tensor(rstd[:, 0:NT], ssq[:, 0:NT], mhalf[:, 0:NT], ALU.pow).then_inc(rstd_done, 1)

            def split(n):
                u = SPLIT[n]
                r = UNIT[u]
                w = 32 if u[0] == "ffng" else P
                pool.wait_ge(raw_landed[r % NRAW], landed(r))
                if n >= NSPLIT:
                    before = SPLIT[n - NSPLIT]
                    if before[0] == "wo":
                        pool.wait_ge(wo_used, before[1] + 1)
                    else:
                        pool.wait_ge(pj_ready, JOB_OF[before] + 1)
                src = raw[:, r % NRAW, :, 0:w]
                hi, lo = w_hi[:, n % NSPLIT, :, 0:w], w_lo[:, n % NSPLIT, :, 0:w]
                link(pool.tensor_copy(hi, src))
                pool.tensor_tensor(lo, src, hi.bitcast(F32), ALU.subtract).then_inc(split_done, 1)

            def rope_rest(job):
                n = ROPEN[job]
                kind, i = job
                pool.wait_ge(t_swapped, 64 * (n + 1))
                pool.wait_ge(pj_dve, emptied("D", JOB[job]))
                link(pool.tensor_tensor(t_swap[:, :], t_swap[:, :], cs[:, 1, :], ALU.mult))
                if kind == "kc":
                    pool.tensor_tensor(t_rope[:, :], t_rope[:, :], t_swap[:, :], ALU.add).then_inc(rope_done, 1)
                    return
                link(pool.tensor_tensor(t_rope[:, :], t_rope[:, :], t_swap[:, :], ALU.add))
                if kind == "nq":
                    pool.wait_ge(s_ready, 3 * (LAST_OF_PAIR[4 + i - 2] + 1))
                    hi, lo = qk_hi[:, i % 2, 0, :], qk_lo[:, i % 2, 0, :]
                else:
                    b = 0 if kind == "ks" else 1
                    hi, lo = nk_hi[:, b, :], nk_lo[:, b, :]
                link(pool.tensor_copy(hi, t_rope[:, :]))
                pool.tensor_tensor(lo, t_rope[:, :], hi.bitcast(F32), ALU.subtract).then_inc(rope_done, 1)

            def blocks(which):
                row = R_PEK if which == 0 else R_PEV
                pool.wait_ge(u_moved, 64 * (which + 1))
                if which:
                    pool.wait_ge(pj_ready, JOB["hidk", 0] + 1)
                for g in range(2):
                    src = bass.AP(tensor=U, offset=g * SEQ,
                                  ap=[[2 * SEQ, P], [2, KC], [CMP_STRIDE, NCMP]])
                    pe = vecsT[:, row:row + KC].unsqueeze(2).to_broadcast([P, KC, NCMP])
                    pool.tensor_tensor(B[:, :, g, :], src, pe, ALU.add).then_inc(b_done, 1)

            pool.wait_ge(rope_in, 16)
            pool.wait_ge(pj_dve, 1)
            for n in range(len(SPLIT)):
                split(n)
                for job in ROPED:
                    if n == SPLITN[job] + (1 if job == ("nq", 3) else 2):
                        rope_rest(job)
                        if job[0] == "kc":
                            blocks(0)
                if SPLIT[n] == ("fk", 3):
                    blocks(1)
            for m in range(NT):
                pool.wait_ge(ovar_done, m + 1)
                pool.tensor_tensor(rstd[:, m:m + 1], ssq[:, 2 * m:2 * m + 1], mhalf[:, 0:1], ALU.pow)\
                    .then_inc(orstd_done, 1)

        @block.scalar
        def _(act):
            act.dma_start(vecs[R_C:R_C + 8, :], c.rearrange("o (r n) -> (o r) n", n=P)).then_inc(vecs_in, 16)
            act.dma_start(vecs[R_GPRE:R_GPRE + 8, :], g_pre.rearrange("o (r n) -> (o r) n", n=P)).then_inc(vecs_in, 16)
            act.dma_start(vecs[R_ADA:R_ADA + 24, :], b_ada.rearrange("o (r n) -> (o r) n", n=P)).then_inc(vecs_in, 16)
            act.dma_start(vecs[R_GPOST:R_GPOST + 8, :], g_post.rearrange("o (r n) -> (o r) n", n=P)).then_inc(vecs_in, 16)
            act.dma_start(vecs[R_PEK:R_PEK + 16, :], pe_cmp_k.rearrange("(r a) n -> r (a n)", a=2)).then_inc(vecs_in, 16)
            act.dma_start(vecs[R_PEV:R_PEV + 16, :], pe_cmp_v.rearrange("(r a) n -> r (a n)", a=2)).then_inc(vecs_in, 16)
            act.dma_start(kon[:, :], consts).then_inc(kon_in, 16)
            for m in range(NT):
                act.dma_start(x_sb[:, m, :], x[m * P:(m + 1) * P, :]).then_inc(x_in[m], 16)
            act.dma_start(cs[:, :, :], rope).then_inc(rope_in, 16)
            act.dma_start(bf[:, :], b_forget.rearrange("o h -> h o")).then_inc(small_in, 16)
            act.dma_start(w2k[:, 0, :], w_cmp_k2).then_inc(small_in, 16)
            act.dma_start(w2k[:, 1, :], w_cmp_k2).then_inc(small_in, 16)
            act.dma_start(w2v[:, :], w_cmp_v2).then_inc(small_in, 16)

            act.wait_ge(pj_dve, 1)
            act.activation(silc[:, 1, :], vecsT[:, R_C:R_C + KD], ACT.Tanh, scale=0.5).then_inc(tanhc_done, 1)
            for m in range(NT):
                act.wait_ge(x_in[m], 16)
                if m:
                    act.wait_ge(sq_done, m)
                act.activation(prob[:, 0, 0:DM], x_sb[:, m, :], ACT.Square,
                               accum_out=ssq[:, m:m + 1]).then_inc(sq_done, 1)

            def move_u(which, src):
                for g in range(2):
                    rows = src[g * HD:(g + 1) * HD, :]
                    act.dma_start(U[0:HD, g, :], rows).then_inc(u_moved, 16)
                    act.dma_start(U[HD:P, g, 0:SEQ - 1], rows[:, 1:SEQ]).then_inc(u_moved, 16)

            t_jobs = [j for j in JOBS if j[0] in ("kc", "ks", "kw", "nq", "vc")]

            def evac(job):
                n = JOB[job]
                kind, i = job
                src = PJ_BANK[n % 2]
                if "A" not in READERS[kind]:
                    return
                act.wait_ge(pj_ready, n + 1)
                if kind == "xT":
                    act.wait_ge(mod_done, 1)
                    act.activation(hT_hi[:, i, :], src[:, :], ACT.Identity, bias=mod[:, i:i + 1],
                                   scale=amul[:, i:i + 1]).then_inc(pj_act, 1)
                elif kind == "vsw":
                    act.activation(vn_hi[:, 2 * i:2 * i + 2, :, :].rearrange("p m b n -> p (m b n)"),
                                   src[:, :], ACT.Copy).then_inc(pj_act, 1)
                elif kind == "fv":
                    half, m2 = i // 2, i % 2
                    act.activation(vf_hi[:, 2 * m2:2 * m2 + 2, 256 * half:256 * half + 256],
                                   src[:, :].rearrange("p (m n) -> p m n", m=2), ACT.Copy).then_inc(pj_act, 1)
                elif kind in ("fq", "fk"):
                    if i >= 2:
                        act.wait_ge(s_ready, 3 * (LAST_OF_PAIR[i - 2] + 1))
                    w = 0 if kind == "fq" else 1
                    act.activation(qk_hi[:, i % 2, w, :], src[:, :], ACT.Copy,
                                   scale=QSCALE if w == 0 else 1.0).then_inc(pj_act, 1)
                elif kind == "ffng":
                    act.activation(gates[:, :, :], src[:, 0:NT * 32].rearrange("p (m n) -> p m n", m=NT)[:, :, 8:32],
                                   ACT.Tanh, scale=0.5).then_inc(pj_act, 1)
                elif kind in ("kc", "ks", "kw", "nq", "vc"):
                    k = t_jobs.index(job)
                    before = t_jobs[:k]
                    if before:
                        act.wait_ge(t_swapped, 64 * sum(j[0] != "vc" for j in before))
                        if ("vc", 0) in before:
                            act.wait_ge(u_moved, 128)
                    act.activation(t_sb[:, :], src[:, :], ACT.Copy,
                                   scale=QSCALE if kind == "nq" else 1.0)\
                       .then_inc(pj_act, 1)
                    act.wait_ge(pj_act, emptied("A", n))
                    if kind == "vc":
                        act.wait_ge(b_done, 2)
                        move_u(1, t_sb)
                    else:
                        r = ROPEN[job]
                        if r:
                            act.wait_ge(rope_done, r)
                        for q in range(4):
                            act.dma_start(t_swap[32 * q:32 * q + 32, :],
                                          t_sb[32 * (q ^ 1):32 * (q ^ 1) + 32, :]).then_inc(t_swapped, 16)
                elif kind in ("fz", "nz"):
                    t = i if kind == "fz" else 4 + i
                    if t >= 2:
                        act.wait_ge(y_done, 2 * (t - 1))
                    act.activation(sz[:, t % 2, :], src[:, :], ACT.Tanh, scale=0.5).then_inc(pj_act, 1)
                elif kind in ("hidk", "hidv"):
                    act.wait_ge(fills_done, 7)
                    if kind == "hidv":
                        act.wait_ge(pj_ready, JOB["kc2", 0] + 1)
                    act.activation(hid[:, :, 0:NCMP], src[:, 0:2 * NCMP].rearrange("p (g n) -> p g n", g=2),
                                   ACT.Tanh, scale=0.5).then_inc(pj_act, 1)
                elif kind == "kc2":
                    act.wait_ge(fills_done, 7)
                    act.activation(kcb_hi[0:HD, 0:NC], src[0:HD, 0:NC], ACT.Copy, scale=0.5)
                    act.activation(kcb_hi[HD:P, NC:2 * NC], src[HD:P, NC:2 * NC], ACT.Copy, scale=0.5)\
                       .then_inc(pj_act, 1)
                elif kind == "vc2":
                    act.activation(vcb[0:NC, 0:HD], src[0:NC, 0:HD], ACT.Copy, scale=0.5)
                    act.activation(vcb[NC:2 * NC, HD:P], src[NC:2 * NC, 0:HD], ACT.Copy, scale=0.5)\
                       .then_inc(pj_act, 1)
                elif kind == "PcT":
                    if i:
                        act.wait_ge(y_ready, 2 * i)
                    act.activation(pcT[:, :], src[0:2 * NC, :], ACT.Copy).then_inc(pj_act, 1)
                elif kind == "gate":
                    act.activation(gg[:, i * P:(i + 1) * P], src[:, P:2 * P], ACT.Copy).then_inc(pj_act, 1)

            def after(job):
                kind, i = job
                if kind == "kc":
                    act.wait_ge(rope_done, 1)
                    move_u(0, t_rope)
                if kind == "ffT":
                    act.wait_ge(ff_abs, 1)
                    act.activation(fe[:, :], fe[:, :], ACT.Exp, scale=-1.0).then_inc(ff_e, 1)
                    act.wait_ge(ff_e, 1)
                    act.activation(fe[:, :], fe[:, :], ACT.Ln, bias=1.0).then_inc(ff_ln, 1)
                    act.wait_ge(ff_cum, 1)
                    act.activation(cum_r[0:8, :], fc[:, :], ACT.Copy, scale=-1.0).then_inc(ff_hi, 1)
                if kind == "Sc":
                    act.wait_ge(c_shift, i + 1)
                    act.activation(pc[:, :, :, :], pc[:, :, :, :], ACT.Exp).then_inc(c_exp, 1)

            for j in PROLOGUE:
                evac(j)
                if j[0] == "ffT":
                    after(j)
                if j == ("fv", 0):
                    after(("kc", 0))

            def exps(s):
                for k, (q, g, col, n) in enumerate(QT):
                    if col == 0:
                        act.wait_ge(max_done, 3 * s + g + 1)
                    if k == 0 and s >= 2:
                        act.wait_ge(pt_ready, 3 * (s - 2) + 3)
                    if k == 0 and s >= 2:
                        act.wait_ge(p_ready, s - 1)
                    last = act.activation(prob[:, s % 2, POFF[q]:POFF[q] + n], S_BANK[g][:, col:col + n], ACT.Exp,
                                          bias=negm[:, s % 2, q:q + 1], scale=1.0,
                                          accum_out=psum_row[:, s % 2, q:q + 1])
                    if k != 1:
                        last.then_inc(exp_done, 1)

            def pt_copy(s, j):
                n = 3 * s + j
                act.wait_ge(pt_ready, n + 1)
                if n >= 3:
                    act.wait_ge(pv_done, n - 2)
                act.activation(pt_hi[:, j, 0:PTW[j]], PT_BANK[n % 2][:, 0:PTW[j]], ACT.Copy).then_inc(pt_hi_done, 1)

            for s in range(NI + 1):
                if s < NI:
                    exps(s)
                if s >= 1:
                    pt_copy(s - 1, 0)
                    pt_copy(s - 1, 1)
                for j in FILL[s] if s < NI else []:
                    evac(j)
                    after(j) if j[0] == "Sc" else None
                if s >= 1:
                    pt_copy(s - 1, 2)

            for t in range(KD):
                act.wait_ge(pj_ready, len(JOBS))
                act.wait_ge(y_done, 2 * t + 2)
                act.activation(hT_hi[:, t, :], y32[:, t, :], ACT.Copy).then_inc(yh_done, 1)
            for m in range(NT):
                for half in range(2):
                    act.wait_ge(o_ready, 2 * m + half + 1)
                    act.wait_ge(yl_done, KD)
                    act.activation(y32[:, 2 * m + half, :], bank[2 * m + half][:, :], ACT.Square,
                                   accum_out=ssq[:, 2 * m + half:2 * m + half + 1]).then_inc(osq_done, 1)

        @block.vector
        def _(dve):
            own = [0]

            def link(ins):
                own[0] += 1
                ins.then_inc(dve_own, 1)
                dve.wait_ge(dve_own, own[0])

            dve.wait_ge(kon_in, 16)
            dve.tensor_copy(ident_r[:, :], ident).then_inc(consts_done, 1)
            dve.tensor_copy(mask_r[:, :], kon[:, K_MASK:K_MASK + P]).then_inc(consts_done, 1)
            dve.tensor_copy(sel_r[:, :], kon[:, K_SEL:K_SEL + 8]).then_inc(consts_done, 1)

            def evac(job):
                n = JOB[job]
                kind, i = job
                src = PJ_BANK[n % 2]
                if "D" not in READERS[kind]:
                    return
                dve.wait_ge(pj_ready, n + 1)
                if "A" in READERS[kind]:
                    dve.wait_ge(pj_act, emptied("A", n))

                def low(dst, hi, frm, scale=1.0):
                    dve.scalar_tensor_tensor(dst, frm, scale, hi.bitcast(F32), ALU.mult, ALU.subtract)\
                       .then_inc(pj_dve, 1)

                if kind == "vecsT":
                    dve.tensor_copy(vecsT[:, :], src[:, 0:R_END]).then_inc(pj_dve, 1)
                    dve.wait_ge(pj_dve, 1)
                    dve.wait_ge(tanhc_done, 1)
                    link(dve.scalar_tensor_tensor(silc[:, 0, :], silc[:, 1, :], 1.0, vecsT[:, R_C:R_C + KD],
                                                  ALU.add, ALU.mult))
                    dve.tensor_scalar(silc[:, 0, :], silc[:, 0, :], 0.5, None, ALU.mult).then_inc(silc_done, 1)
                    dve.wait_ge(sq_done, NT)
                    dve.tensor_scalar(ssq[:, 0:NT], ssq[:, 0:NT], 1.0 / DM, EPS, ALU.mult, ALU.add).then_inc(var_done, 1)
                    dve.wait_ge(rstd_done, 1)
                    for m in range(NT):
                        dve.tensor_scalar(x_sb[:, m, :], x_sb[:, m, :], rstd[:, m:m + 1], None, ALU.mult)\
                           .then_inc(xn_done, 1)
                elif kind == "ada":
                    dve.tensor_tensor(mod[:, :], src[:, 0:16], vecsT[:, R_ADA:R_ADA + 16], ALU.add).then_inc(pj_dve, 1)
                    dve.wait_ge(pj_dve, 2)
                    dve.scalar_tensor_tensor(amul[:, :], mod[:, 8:16], 1.0, vecsT[:, R_GPRE:R_GPRE + 8],
                                             ALU.add, ALU.mult).then_inc(mod_done, 1)
                    dve.wait_ge(mod_done, 1)
                elif kind == "xT":
                    link(dve.tensor_scalar(t_rope[:, :], src[:, :], amul[:, i:i + 1], mod[:, i:i + 1],
                                           ALU.mult, ALU.add))
                    dve.tensor_tensor(hT_lo[:, i, :], t_rope[:, :], hT_hi[:, i, :].bitcast(F32), ALU.subtract)\
                       .then_inc(pj_dve, 1)
                    dve.wait_ge(pj_dve, emptied("D", n))
                elif kind == "vsw":
                    low(vn_lo[:, 2 * i:2 * i + 2, :, :].rearrange("p m b n -> p (m b n)"),
                        vn_hi[:, 2 * i:2 * i + 2, :, :].rearrange("p m b n -> p (m b n)"), src[:, :])
                elif kind == "fv":
                    half, m2 = i // 2, i % 2
                    low(vf_lo[:, 2 * m2:2 * m2 + 2, 256 * half:256 * half + 256],
                        vf_hi[:, 2 * m2:2 * m2 + 2, 256 * half:256 * half + 256],
                        src[:, :].rearrange("p (m n) -> p m n", m=2))
                elif kind in ("fq", "fk"):
                    w = 0 if kind == "fq" else 1
                    low(qk_lo[:, i % 2, w, :], qk_hi[:, i % 2, w, :], src[:, :], QSCALE if w == 0 else 1.0)
                elif kind == "ffng":
                    dve.tensor_copy(ffc[:, :, :], src[:, 0:NT * 32].rearrange("p (m n) -> p m n", m=NT)[:, :, 0:8])\
                       .then_inc(pj_dve, 1)
                    dve.tensor_scalar(gates[:, :, :], gates[:, :, :], 1.0, 0.5, ALU.add, ALU.mult).then_inc(gates_done, 1)
                elif kind in ("kc", "ks", "kw", "nq"):
                    r = ROPEN[job]
                    dve.wait_ge(rope_in, 16)
                    if r:
                        dve.wait_ge(rope_done, r)
                    if r == 1:
                        dve.wait_ge(u_moved, 64)
                    dve.scalar_tensor_tensor(t_rope[:, :], src[:, :], QSCALE if kind == "nq" else 1.0, cs[:, 0, :],
                                             ALU.mult, ALU.mult).then_inc(pj_dve, 1)
                elif kind == "ffT":
                    dve.wait_ge(small_in, 64)
                    dve.wait_ge(fills_done, 7)
                    dve.tensor_scalar(fz[:, :], src[0:8, :], bf[:, 0:1], None, ALU.add).then_inc(pj_dve, 1)
                    dve.wait_ge(pj_dve, emptied("D", n))
                    dve.scalar_tensor_tensor(fe[:, :], fz[:, :], -1.0, fz[:, :], ALU.mult, ALU.max).then_inc(ff_abs, 1)
                    dve.wait_ge(ff_ln, 1)
                    link(dve.scalar_tensor_tensor(fz[:, :], fz[:, :], 0.0, fe[:, :], ALU.min, ALU.subtract))
                    dve.tensor_tensor_scan(fc[:, :], fo[:, :], fz[:, :], 0.0, ALU.mult, ALU.add).then_inc(ff_cum, 1)
                    dve.wait_ge(ff_hi, 1)
                    dve.scalar_tensor_tensor(cum_r[32:40, :], fc[:, :], -1.0, cum_r[0:8, :].bitcast(F32),
                                             ALU.mult, ALU.subtract).then_inc(ff_lo, 1)
                elif kind in ("fz", "nz"):
                    t = i if kind == "fz" else 4 + i
                    dve.scalar_tensor_tensor(sz[:, t % 2, :], sz[:, t % 2, :], 1.0, src[:, :], ALU.add, ALU.mult)\
                       .then_inc(pj_dve, 1)
                elif kind in ("hidk", "hidv"):
                    dve.scalar_tensor_tensor(hid[:, :, 0:NCMP], hid[:, :, 0:NCMP], 1.0,
                                             src[:, 0:2 * NCMP].rearrange("p (g n) -> p g n", g=2),
                                             ALU.add, ALU.mult).then_inc(pj_dve, 1)
                elif kind == "kc2":
                    dve.scalar_tensor_tensor(kcb_lo[0:HD, 0:NC], src[0:HD, 0:NC], 0.5,
                                             kcb_hi[0:HD, 0:NC].bitcast(F32), ALU.mult, ALU.subtract)
                    dve.scalar_tensor_tensor(kcb_lo[HD:P, NC:2 * NC], src[HD:P, NC:2 * NC], 0.5,
                                             kcb_hi[HD:P, NC:2 * NC].bitcast(F32), ALU.mult, ALU.subtract)\
                       .then_inc(pj_dve, 1)
                elif kind == "Sc":
                    compressed(i, src)
                elif kind == "gate":
                    dve.tensor_tensor(gg[:, i * P:(i + 1) * P], src[:, 0:P], gg[:, i * P:(i + 1) * P], ALU.mult)\
                       .then_inc(pj_dve, 1)

            def compressed(i, src):
                s3 = src[:, 0:NT * 2 * NC].rearrange("p (m a n) -> p m a n", m=NT, a=2)
                rows = pcs[:, 0, :].rearrange("p (m a) -> p m a", m=NT)
                cmask = kon[:, K_CMASK:K_CMASK + NT * NC].rearrange("p (m n) -> p m n", m=NT)
                if i:
                    dve.wait_ge(pj_ready, JOB["PcT", i - 1] + 1)
                last = [dve.tensor_tensor(pc[:, :, a, :], s3[:, :, a, :], cmask, ALU.add) for a in range(2)][-1]
                last.then_inc(pj_dve, 1)
                dve.wait_ge(pj_dve, emptied("D", JOB["Sc", i]))
                link(dve.tensor_reduce(rows, pc[:, :, :, :], AX_X, ALU.max))
                link(dve.tensor_scalar(rows, rows, NEG / 10, None, ALU.max))
                flat = pc[:, :, :, :].rearrange("p m a n -> p (m a) n")
                dve.tensor_tensor(flat, flat, pcs[:, 0, :].unsqueeze(2).to_broadcast([P, 2 * NT, NC]),
                                  ALU.subtract).then_inc(c_shift, 1)
                dve.wait_ge(c_exp, i + 1)
                link(dve.tensor_reduce(pcs[:, 1, :].rearrange("p (m a) -> p m a", m=NT), pc[:, :, :, :], AX_X, ALU.add))
                link(dve.tensor_scalar(pcs[:, 1, :], pcs[:, 1, :], 1e-30, None, ALU.max))
                link(dve.reciprocal(pcs[:, 2, :], pcs[:, 1, :]))
                g = bass.AP(tensor=gates, offset=3 * i, ap=[[NT * 24, P], [24, NT], [12, 2]])
                r = pcs[:, 2, :].rearrange("p (m a) -> p m a", m=NT)
                link(dve.tensor_tensor(r, r, g, ALU.mult))
                dve.tensor_tensor(flat, flat, pcs[:, 2, :].unsqueeze(2).to_broadcast([P, 2 * NT, NC]),
                                  ALU.mult).then_inc(c_prob, 1)

            for j in PROLOGUE:
                evac(j)

            def maxima(s):
                if s >= 2:
                    dve.wait_ge(exp_done, 3 * (s - 1))
                for k, (q, g, col, n) in enumerate(QT):
                    if col == 0:
                        dve.wait_ge(s_ready, 3 * s + g + 1)
                    last = dve.tensor_reduce(negm[:, s % 2, q:q + 1], S_BANK[g][:, col:col + n], AX_X, ALU.max,
                                             negate=True)
                    if k != 1:
                        last.then_inc(max_done, 1)

            def y_out(s):
                p, a, _ = INST[s]
                h = head_of(s)
                r = slice(HD * a, HD * a + HD)
                if h < FOX_H:
                    dve.wait_ge(pv_done, 3 * s + 3)
                else:
                    dve.wait_ge(y_ready, h - FOX_H + 1)
                dve.scalar_tensor_tensor(y32[r, p, :], Y_BANK[r, :], 0.5, sz[r, p % 2, :], ALU.mult, ALU.mult)\
                   .then_inc(y_done, 1)

            def pt_low(s, j):
                n = 3 * s + j
                dve.wait_ge(pt_hi_done, n + 1)
                dve.tensor_tensor(pt_lo[:, j, 0:PTW[j]], PT_BANK[n % 2][:, 0:PTW[j]],
                                  pt_hi[:, j, 0:PTW[j]].bitcast(F32), ALU.subtract).then_inc(pt_lo_done, 1)

            def normalise(s):
                p, a, b = INST[s]
                dve.wait_ge(exp_done, 3 * s + 3)
                r = rinv[:, s % 2, :]
                link(dve.reciprocal(r, psum_row[:, s % 2, :]))
                if b is not None:
                    col = 3 * (p - 4 + 4 * a) + 1 + b
                    g = bass.AP(tensor=gates, offset=col, ap=[[NT * 24, P], [24, NT]])
                    link(dve.tensor_tensor(r, r, g, ALU.mult))
                for q, _, _, n in QT:
                    last = dve.tensor_scalar(prob[:, s % 2, POFF[q]:POFF[q] + n], prob[:, s % 2, POFF[q]:POFF[q] + n],
                                             rinv[:, s % 2, q:q + 1], None, ALU.mult)
                last.then_inc(p_ready, 1)

            dve.wait_ge(gates_done, 1)
            for s in range(NI + 2):
                if s < NI:
                    maxima(s)
                if s >= 2 and last_of_head(s - 2):
                    y_out(s - 2)
                if 1 <= s <= NI:
                    pt_low(s - 1, 0)
                    pt_low(s - 1, 1)
                for j in FILL[s] if s < NI else []:
                    evac(j)
                if 1 <= s <= NI:
                    pt_low(s - 1, 2)
                if s < NI:
                    normalise(s)

            for t in range(KD):
                dve.wait_ge(yh_done, t + 1)
                dve.tensor_tensor(hT_lo[:, t, :], y32[:, t, :], hT_hi[:, t, :].bitcast(F32), ALU.subtract)\
                   .then_inc(yl_done, 1)
            for m in range(NT):
                pair = ssq[:, 2 * m:2 * m + 2]
                dve.wait_ge(osq_done, 2 * m + 2)
                link(dve.tensor_tensor(ssq[:, 2 * m:2 * m + 1], pair[:, 0:1], pair[:, 1:2], ALU.add))
                dve.tensor_scalar(ssq[:, 2 * m:2 * m + 1], ssq[:, 2 * m:2 * m + 1], 1.0 / DM, EPS, ALU.mult, ALU.add)\
                   .then_inc(ovar_done, 1)
                dve.wait_ge(orstd_done, m + 1)
                dve.wait_ge(xres_in, 16 * NT)
                for half in range(2):
                    cols = slice(512 * half, 512 * half + 512)
                    w = prob[:, m % 2, cols]
                    link(dve.scalar_tensor_tensor(w, bank[2 * m + half][:, :], rstd[:, m:m + 1], gg[:, cols],
                                                  ALU.mult, ALU.mult))
                    dve.tensor_tensor(x_res[:, m, cols], x_res[:, m, cols], w, ALU.add).then_inc(o_done, 1)

        @block.tensor
        def _(pe):
            def mm3(dst, l_hi, l_lo, r_hi, r_lo, start, stop):
                pe.matmul(dst, l_hi, r_hi, start=start, stop=False)
                pe.matmul(dst, l_hi, r_lo, start=False, stop=False)
                return pe.matmul(dst, l_lo, r_hi, start=False, stop=stop)

            def wait_raw(u):
                pe.wait_ge(raw_landed[UNIT[u] % NRAW], landed(UNIT[u]))
                return UNIT[u] % NRAW

            def wait_split(u):
                pe.wait_ge(split_done, SPLITN[u] + 1)
                return SPLITN[u] % NSPLIT

            def job(j):
                n = JOB[j]
                kind, i = j
                dst = PJ_BANK[n % 2]
                if n >= 2:
                    a, d = emptied("A", n - 2), emptied("D", n - 2)
                    if a:
                        pe.wait_ge(pj_act, a)
                    if d:
                        pe.wait_ge(pj_dve, d)
                if kind == "vecsT":
                    pe.wait_ge(vecs_in, 96)
                    pe.wait_ge(kon_in, 16)
                    pe.transpose(dst[:, 0:R_END], vecs[:, :], ident[0:R_END, 0:R_END]).then_inc(pj_ready, 1)
                elif kind == "ada":
                    pe.wait_ge(silc_done, 1)
                    for u in range(16):
                        slot = wait_raw(("ada", u))
                        for k in range(KD):
                            last = pe.matmul(dst[:, u:u + 1], raw[:, slot, k, :], silc[:, 0, k:k + 1],
                                             start=(k == 0), stop=(k == KD - 1))
                        last.then_inc(raw_used if u < 15 else pj_ready, 1)
                elif kind == "xT":
                    pe.wait_ge(xn_done, NT)
                    for m in range(NT):
                        last = pe.transpose(dst[:, m * P:(m + 1) * P], x_sb[:, m, i * P:(i + 1) * P], ident)
                    last.then_inc(pj_ready, 1)
                elif kind in ("vsw", "fv"):
                    if kind == "vsw":
                        wait_split(("vs", 0))
                        slot = wait_split(("vw", 0)) - 1
                        m2 = i
                        pe.wait_ge(pj_dve, emptied("D", JOB["xT", KD - 1]))
                    else:
                        half, m2 = i // 2, i % 2
                        slot = wait_split(("fv", 2 * half + 1)) - 1
                    for m in range(2):
                        tok = slice((2 * m2 + m) * P, (2 * m2 + m + 1) * P)
                        for k in range(KD):
                            last = mm3(dst[:, 256 * m:256 * m + 256], hT_hi[:, k, tok], hT_lo[:, k, tok],
                                       w_hi[:, slot:slot + 2, k, :], w_lo[:, slot:slot + 2, k, :],
                                       k == 0, k == KD - 1)
                    last.then_inc(pj_ready, 1)
                elif kind == "ffng":
                    slot = wait_split(j)
                    for m in range(NT):
                        tok = slice(m * P, (m + 1) * P)
                        for k in range(KD):
                            last = mm3(dst[:, 32 * m:32 * m + 32], hT_hi[:, k, tok], hT_lo[:, k, tok],
                                       w_hi[:, slot, k, 0:32], w_lo[:, slot, k, 0:32], k == 0, k == KD - 1)
                    last.then_inc(pj_ready, 1)
                elif kind == "ffT":
                    pe.wait_ge(pj_dve, emptied("D", JOB["ffng", 0]))
                    for m in range(NT):
                        last = pe.transpose(dst[0:8, m * P:(m + 1) * P], ffc[:, m, :], ident)
                    last.then_inc(pj_ready, 1)
                elif kind in ("kc", "fq", "fk", "fz", "vc", "ks", "nq", "kw", "nz"):
                    slot = wait_split(j)
                    for k in range(KD):
                        last = mm3(dst[:, :], w_hi[:, slot, k, :], w_lo[:, slot, k, :], hT_hi[:, k, :], hT_lo[:, k, :],
                                   k == 0, k == KD - 1)
                    last.then_inc(pj_ready, 1)
                elif kind in ("hidk", "hidv"):
                    pe.wait_ge(b_done, 2 if kind == "hidk" else 4)
                    for kk in range(KC):
                        if kk % 8 == 0:
                            slot = wait_raw((kind, kk // 8))
                        last = pe.matmul(dst[:, 0:2 * NCMP], raw[:, slot, kk % 8, :],
                                         B[:, kk, :, :].rearrange("p g n -> p (g n)"),
                                         start=(kk == 0), stop=(kk == KC - 1))
                        if kk == 7:
                            last.then_inc(raw_used, 1)
                    last.then_inc(pj_ready, 1)
                elif kind in ("kc2", "vc2"):
                    pe.wait_ge(small_in, 64)
                    pe.wait_ge(pj_dve, emptied("D", JOB["hidk" if kind == "kc2" else "hidv", 0]))
                    h2 = hid[:, :, :].rearrange("p g n -> p (g n)")
                    if kind == "kc2":
                        pe.matmul(dst[:, 0:2 * NC], w2k[:, :, :].rearrange("p a n -> p (a n)"), h2,
                                  start=True, stop=True).then_inc(pj_ready, 1)
                    else:
                        pe.matmul(dst[0:2 * NC, 0:HD], h2, w2v[:, :], start=True, stop=True).then_inc(pj_ready, 1)
                elif kind == "Sc":
                    pe.wait_ge(rope_done, ROPEN["nq", i] + 1)
                    pe.wait_ge(pj_dve, emptied("D", JOB["kc2", 0]))
                    for m in range(NT):
                        tok = slice(m * P, (m + 1) * P)
                        last = mm3(dst[:, 64 * m:64 * m + 64], qk_hi[:, i % 2, 0, tok], qk_lo[:, i % 2, 0, tok],
                                   kcb_hi[:, :], kcb_lo[:, :], True, True)
                    last.then_inc(pj_ready, 1)
                elif kind == "PcT":
                    pe.wait_ge(c_prob, i + 1)
                    for m in range(NT):
                        last = pe.transpose(dst[0:2 * NC, m * P:(m + 1) * P],
                                            pc[:, m, :, :].rearrange("p a n -> p (a n)"), ident)
                    last.then_inc(pj_ready, 1)
                elif kind == "gate":
                    slot = wait_raw(j)
                    for k in range(KD):
                        pe.matmul(dst[:, 0:P], silc[:, 0, k:k + 1].to_broadcast([P, P]), raw[:, slot, k, :],
                                  start=(k == 0), stop=False)
                    r = R_ADA + 16 + i
                    pe.matmul(dst[:, 0:P], ident[0:R_END, r:r + 1].to_broadcast([R_END, P]), vecs[:, :],
                              start=False, stop=True)
                    r = R_GPOST + i
                    pe.matmul(dst[:, P:2 * P], ident[0:R_END, r:r + 1].to_broadcast([R_END, P]), vecs[:, :],
                              start=True, stop=True).then_inc(pj_ready, 1)


            def scores(s):
                p, a, b = INST[s]
                r = slice(HD * a, HD * a + HD)
                slot = p % 2
                if b is None:
                    pe.wait_ge(pj_dve, emptied("D", JOB["fk", p]))
                    k_hi, k_lo = qk_hi[r, slot, 1, :], qk_lo[r, slot, 1, :]
                else:
                    pe.wait_ge(rope_done, 1 + max(ROPEN["nq", p - 4], ROPEN["ks" if b == 0 else "kw", 0]))
                    k_hi, k_lo = nk_hi[r, b, :], nk_lo[r, b, :]
                if s == 0:
                    pe.wait_ge(consts_done, 3)
                    pe.wait_ge(ff_lo, 1)
                for k, (q, g, col, n) in enumerate(QT):
                    if col == 0 and s >= 1:
                        pe.wait_ge(exp_done, 3 * (s - 1) + g + 1)
                    dst = S_BANK[g]
                    tok = slice(q * P, (q + 1) * P)
                    mm3(dst[:, col:col + n], qk_hi[r, slot, 0, tok], qk_lo[r, slot, 0, tok], k_hi[:, 0:n], k_lo[:, 0:n],
                        True, False)
                    if b is None:
                        h = head_of(s)
                        pe.matmul(dst[:, col:col + n], sel_r[:, h:h + 1].to_broadcast([P, P]), cum_r[:, 0:n],
                                  start=False, stop=False)
                    last = pe.matmul(dst[:, col + n - P:col + n], ident_r[:, :], mask_r[:, :], start=False, stop=True)
                    if k != 1:
                        last.then_inc(s_ready, 1)

            def transposes(s, j):
                n = 3 * s + j
                if j == 0:
                    pe.wait_ge(p_ready, s + 1)
                if n >= 2:
                    pe.wait_ge(pt_lo_done, n - 1)
                for kt, col in PTG[j]:
                    for q in range(kt, NT):
                        o = POFF[q] + kt * P
                        last = pe.transpose(PT_BANK[n % 2][:, col + (q - kt) * P:col + (q - kt + 1) * P],
                                            prob[:, s % 2, o:o + P], ident)
                last.then_inc(pt_ready, 1)

            def values(s, j):
                p, a, b = INST[s]
                h = head_of(s)
                pe.wait_ge(pt_lo_done, 3 * s + j + 1)
                if first_of_head(s) and j == 0 and h:
                    pe.wait_ge(y_done, h)
                for kt, col in PTG[j]:
                    w = SEQ - kt * P
                    if b is None:
                        v_hi, v_lo = vf_hi[:, kt, P * p:P * p + P], vf_lo[:, kt, P * p:P * p + P]
                    else:
                        v_hi, v_lo = vn_hi[:, kt, b, :], vn_lo[:, kt, b, :]
                    last = mm3(Y_BANK[:, kt * P:SEQ], v_hi, v_lo, pt_hi[:, j, col:col + w], pt_lo[:, j, col:col + w],
                               first_of_head(s) and j == 0, b is None and j == 2)
                last.then_inc(pv_done, 1)
                if b is not None and last_of_head(s) and j == 2:
                    g = slice(NC * a, NC * a + NC)
                    pe.wait_ge(pj_act, emptied("A", JOB["PcT", p - 4]))
                    pe.matmul(Y_BANK[:, :], vcb[g, :], pcT[g, :], start=False, stop=True).then_inc(y_ready, 1)

            for j in PROLOGUE:
                job(j)
            for s in range(NI + 2):
                if s < NI:
                    scores(s)
                if s >= 2:
                    values(s - 2, 2)
                if 1 <= s <= NI:
                    transposes(s - 1, 0)
                    transposes(s - 1, 1)
                for j in FILL[s] if s < NI else []:
                    job(j)
                if 1 <= s <= NI:
                    values(s - 1, 0)
                    transposes(s - 1, 2)
                    values(s - 1, 1)

            for kt in range(KD):
                slot = wait_split(("wo", kt))
                pe.wait_ge(yl_done, kt + 1)
                if kt == 0:
                    pe.wait_ge(exp_done, 3 * NI)
                    pe.wait_ge(pt_lo_done, 3 * NI)
                    pe.wait_ge(y_done, FOX_H + NSA_H)
                    pe.wait_ge(pj_act, emptied("A", len(JOBS) - 1))
                    pe.wait_ge(pj_dve, emptied("D", len(JOBS) - 1))
                for m in range(NT):
                    tok = slice(m * P, (m + 1) * P)
                    for half in range(2):
                        w = slice(4 * half, 4 * half + 4)
                        last = mm3(bank[2 * m + half][:, :], hT_hi[:, kt, tok], hT_lo[:, kt, tok],
                                   w_hi[:, slot, w, :], w_lo[:, slot, w, :], kt == 0, kt == KD - 1)
                        if kt == KD - 1:
                            last.then_inc(o_ready, 1)
                if kt < KD - 1:
                    last.then_inc(wo_used, 1)


_INS = ["x", "c", "g_pre", "g_post", "w_ada", "b_ada", "w_in", "b_forget", "w_cmp_k1", "w_cmp_k2",
        "w_cmp_v1", "w_cmp_v2", "pe_cmp_k", "pe_cmp_v", "w_out"]
_STACKED = ("w_ada", "w_in", "w_cmp_k1", "w_cmp_k2", "w_cmp_v1", "w_cmp_v2", "pe_cmp_k", "pe_cmp_v", "w_out")


def _rope_tables():
    import numpy as np
    inv = (1.0 / (np.float32(10000.0) ** (np.arange(0, HD, 2, dtype=np.float32) / np.float32(HD)))).astype(np.float32)
    ang = np.arange(SEQ, dtype=np.float32)[:, None] * inv[None, :]
    cos, sin = np.cos(ang).T, np.sin(ang).T
    return np.ascontiguousarray(np.stack([np.tile(cos, (4, 1)), np.concatenate([-sin, sin, -sin, sin])], 1).astype(np.float32))


def _constants():
    import numpy as np
    k = np.zeros((P, K_END), np.float32)
    k[:, K_ID:K_ID + P] = np.eye(P)
    row = np.arange(P)
    k[:, K_MASK:K_MASK + P] = np.where(row[None, :] <= row[:, None], 0.0, NEG)
    n = np.arange(NC)
    for m in range(NT):
        seen = (n[None, :] * CMP_STRIDE + CMP_BLOCK - 1 <= m * P + row[:, None]) & (n[None, :] < NCMP)
        k[:, K_CMASK + m * NC:K_CMASK + (m + 1) * NC] = np.where(seen, 0.0, NEG)
    for h in range(8):
        k[h, K_SEL + h] = k[32 + h, K_SEL + h] = 1.0
    return k


def kernel(**inputs):
    import numpy as _np
    import concourse.bacc as _bacc
    from concourse import mybir as _mybir
    from concourse.bass_utils import run_bass_kernel_spmd as _run

    nc = _bacc.Bacc("TRN2", target_bir_lowering=False, num_devices=1)
    given = {}
    for name in _INS:
        a = _np.ascontiguousarray(inputs[name])
        given[name] = a[0] if name in _STACKED or name == "x" else a
    given["rope"], given["consts"] = _rope_tables(), _constants()
    arrays, args = {}, []
    for name, a in given.items():
        arrays[f"in_{name}_dram"] = a
        args.append(nc.dram_tensor(f"in_{name}_dram", a.shape, _mybir.dt.from_np(a.dtype), kind="ExternalInput").ap())
    args.append(nc.dram_tensor("out_0_dram", (SEQ, DM), _mybir.dt.float32, kind="ExternalOutput").ap())
    hybrid_layer_kernel(nc, *args)
    r = _run(nc, [arrays], core_ids=[0])
    return r.results[0]["out_0_dram"].reshape(1, SEQ, DM)
```

```python
from contextlib import ExitStack

import concourse.bass as bass
from concourse import mybir

F32 = mybir.dt.float32
R32 = mybir.dt.float32r
ALU = mybir.AluOpType
ACT = mybir.ActivationFunctionType
AX_X = mybir.AxisListType.X

P = 128
SEQ = 512
DM = 1024
HD = 64
NT = SEQ // P
KD = DM // P
FOX_W = DM // 2
FOX_H = FOX_W // HD
NSA_H = FOX_H
KV_W = 2 * HD
CMP_BLOCK, CMP_STRIDE = 32, 16
NCMP = (SEQ - CMP_BLOCK) // CMP_STRIDE + 1
NC = NCMP + 1
KC = CMP_BLOCK * HD // P
EPS = 1e-6
NEG = -1.0e30
QSCALE = HD ** -0.5

C_FQ, C_FK, C_FV, C_FF = 0, FOX_W, 2 * FOX_W, 3 * FOX_W
C_FZ = C_FF + FOX_H
C_NQ = C_FZ + FOX_W
C_KC = C_NQ + FOX_W
C_VC, C_KS, C_VS, C_KW, C_VW = (C_KC + i * KV_W for i in range(1, 6))
C_NG = C_KC + 6 * KV_W
C_NZ = C_NG + 3 * NSA_H

R_C, R_GPRE, R_ADA, R_GPOST, R_PEK, R_PEV, R_END = 0, 8, 16, 40, 48, 64, 80

K_ID, K_MASK, K_CMASK, K_SEL, K_END = 0, 128, 256, 256 + NT * NC, 256 + NT * NC + 8

ORDER = [0, 4, 1, 5, 2, 6, 7, 3]
PLACE = {p: k for k, p in enumerate(ORDER)}

EARLY_X = 6
H_ORDER = [d % KD for d in range(EARLY_X, EARLY_X + KD)]
SIDE = [11, 12, 13, 14, 15]
SIDE_BEHIND = [0, 1, 7, 9, 10]
ADA_ORDER = [0, 1, 2, 3, 11, 4, 5, 12, 6, 7, 13, 8, 9, 14, 10, 15]
PROLOGUE = [("ada", n) for n in ADA_ORDER] + [("xT", d) for d in range(EARLY_X, KD)] + [
    ("kc", 0), ("ffng", 0), ("vsw", 0), ("ngT", 0), ("vsw", 1), ("fv", 0), ("fv", 1), ("ks", 0), ("fq", 0), ("fk", 0),
    ("nq", 0)]
MEAN_SQUARES_AT, SCALE_X_AT, EARLY_X_AT = 6, 9, 12
ROOTS_BEFORE = 3
FILL = [
    [("fz", 0)], [("kw", 0), ("vc", 0)],
    [("hidk", 0), ("fq", 1), ("kc2", 0)], [("hidv", 0), ("Sc", 0)], [("vc2", 0), ("nz", 0), ("PcT", 0)], [("fk", 1)],
    [("nq", 1)], [("fz", 1)],
    [("Sc", 1), ("fq", 2)], [("PcT", 1), ("nz", 1)], [("fk", 2)], [("fv", 2)],
    [("fv", 3), ("nq", 2)], [("fz", 2)],
    [("Sc", 2), ("nz", 2)], [("PcT", 2), ("nq", 3)], [("gate", 0), ("gate", 1)], [("nz", 3)],
    [("Sc", 3), ("fq", 3)], [("PcT", 3), ("fk", 3)], [("gate", 2), ("gate", 3)], [("fz", 3)],
    [], [],
]
JOBS = PROLOGUE + [j for f in FILL for j in f]
JOB = {j: n for n, j in enumerate(JOBS)}
READERS = dict(ada="D", xT="A", vsw="AD", ffng="AD", kc="AD", ngT="D", fv="AD", fq="AD",
               fk="AD", fz="AD", vc="A", hidk="AD", hidv="AD", kc2="AD", vc2="AD", ks="AD", nq="AD",
               kw="AD", nz="AD", Sc="D", PcT="AD", gate="AD")


def emptied(who, n):
    return sum(who in READERS[k] for k, _ in JOBS[:n + 1])


NRAW, NSPLIT, NSUM = 4, 4, 4


def units_of(job):
    kind, i = job
    if kind == "ada" and i in SIDE:
        return []
    if kind == "vsw":
        return [("vs", 0), ("vw", 0)] if i == 0 else []
    if kind == "fv":
        return [("fv", i), ("fv", i + 1)] if i in (0, 2) else []
    if kind in ("hidk", "hidv"):
        return [(kind, 0), (kind, 1)]
    if kind == "gate":
        return [("gate", 2 * i), ("gate", 2 * i + 1)]
    if kind in ("ada", "ffng", "kc", "fq", "fk", "fz", "vc", "ks", "nq", "kw", "nz"):
        return [job]
    return []


UNITS = [u for j in JOBS for u in units_of(j)] + [("wo", k) for k in range(KD)]
UNIT = {u: n for n, u in enumerate(UNITS)}
DIRECT = ("ada", "hidk", "hidv")
PREP = [u for u in UNITS if u[0] not in DIRECT]
SPLIT = [u for u in PREP if u[0] != "gate"]
SPLITN = {u: n for n, u in enumerate(SPLIT)}
TWO = ("ffng", "nq", "nz")


def dmas_of(u):
    return 2 if u[0] in TWO or (u[0] == "wo" and ORDER[u[1]] >= KD // 2) else 1


def landed(n):
    return 16 * sum(dmas_of(UNITS[m]) for m in range(n % NRAW, n + 1, NRAW))


JOB_OF = {u: JOB[j] for j in JOBS for u in units_of(j)}
JOB_OF["fv", 0], JOB_OF["fv", 1] = JOB["fv", 1], JOB["fv", 1]
JOB_OF["fv", 2], JOB_OF["fv", 3] = JOB["fv", 3], JOB["fv", 3]
JOB_OF["vs", 0], JOB_OF["vw", 0] = JOB["vsw", 1], JOB["vsw", 1]
ROPED = [j for j in JOBS if j[0] in ("kc", "ks", "kw", "nq")]
ROPEN = {j: n for n, j in enumerate(ROPED)}
MIDJOB = [("hidk", 0), ("hidv", 0)]


def plan():
    vector, gpsimd = {}, {}
    nxt, prod, gate = 0, 0, 0
    prod_at = []
    free_at = {}
    for n, j in enumerate(JOBS):
        vector[j], gpsimd[j] = [], []
        for u in UNITS:
            if u[0] in DIRECT and JOB_OF[u] == n:
                free_at[u] = n
        if j in ROPED:
            gpsimd[j].append(("rope", j))
        if n < len(ADA_ORDER) - 2:
            continue

        def refilled(u):
            lag = 2 if n < JOB["kc", 0] else 1
            return all(free_at.get(b, len(JOBS)) + lag <= n for b in UNITS[:max(UNIT[u] - NRAW + 1, 0)])

        while gate < prod and prod_at[gate] < n and (gate < NSUM or JOB["gate", (gate - NSUM) // 2] <= n):
            vector[j].append(("gate", gate))
            free_at["gate", gate] = n
            gate += 1
        for _ in range(3 if n >= len(ADA_ORDER) else 1):
            if ("gate", prod) in UNIT and refilled(("gate", prod)):
                gpsimd[j].append(("gate", prod))
                prod_at.append(n)
                prod += 1
            u = SPLIT[nxt] if nxt < len(SPLIT) else None
            if u is None or not refilled(u):
                continue
            if SPLITN[u] >= NSPLIT:
                before = SPLIT[SPLITN[u] - NSPLIT]
                if before[0] == "wo" or JOB_OF[before] > n:
                    continue
            vector[j].append(u)
            gpsimd[j].append(u)
            free_at[u] = n
            nxt += 1
    return vector, gpsimd, SPLIT[nxt:]


PREP_AFTER, POOL_AFTER, PREP_LAST = plan()
assert all(SPLITN[u] % NSPLIT < NSPLIT - 1 for u in (("vs", 0), ("fv", 0), ("fv", 2)))
assert all(JOB_OF[u] > n for n, j in enumerate(JOBS) for u in PREP_AFTER[j] if u in JOB_OF)


INST = [(p, a, b) for p in ORDER for a in range(2) for b in ((None,) if p < 4 else (0, 1))]
NI = len(INST)
LAST_H = JOB["fz", 3]
Y_SPLIT = {21: (0, 1), 22: (2, 3), 23: (4, 5), 24: (6,), 25: (7,)}
EARLY_OUT = {22: [(0, 3), (1, 3)], 23: [(2, 3), (3, 3)], 24: [(0, 0), (1, 0)]}
LATER_OUT = [(2, 0), (3, 0)] + [(kt, m) for kt in range(KD // 2) for m in (1, 2)]
LAST_STEP = [max(s for s, i in enumerate(INST) if i[0] == p) for p in ORDER]
QT = [(3, 0, 0, 512), (2, 1, 0, 384), (0, 1, 384, 128), (1, 2, 0, 256)]
POFF = {q: g * 512 + c for q, g, c, _ in QT}
PTG = [[(0, 0)], [(1, 0), (3, 384)], [(2, 0)]]
PTW = [512, 512, 256]


def head_of(s):
    p, a, _ = INST[s]
    return 2 * p + a


def heads_before(s):
    p, a, _ = INST[s]
    return 2 * PLACE[p] + a


def first_of_head(s):
    return INST[s][2] in (None, 0)


def last_of_head(s):
    return INST[s][2] in (None, 1)


def hybrid_layer_kernel(nc, x, w_ada, w_in, b_forget, w_cmp_k1, w_cmp_k2, w_cmp_v1, w_cmp_v2, w_out,
                        vec_rows, vec_cols, rope, consts, out):
    with ExitStack() as ctx:
        def sb(name, shape, dt=F32, scope=None):
            return (scope or ctx).enter_context(nc.sbuf_tensor(name, shape, dt))

        def sem(name):
            return ctx.enter_context(nc.semaphore(name))

        bank = [ctx.enter_context(nc.psum_tensor(f"bank{i}", [P, 512], F32)) for i in range(8)]
        S_BANK, PT_BANK, Y_BANK, PJ_BANK = bank[0:3], bank[3:5], bank[5], bank[6:8]

        hT_hi = sb("hT_hi", [P, KD, SEQ], R32)
        hT_lo = sb("hT_lo", [P, KD, SEQ], R32)
        raw = sb("raw", [P, NRAW, KD, P])
        w_hi = sb("w_hi", [P, NSPLIT, KD, P], R32)
        w_lo = sb("w_lo", [P, NSPLIT, KD, P], R32)
        nk_hi = sb("nk_hi", [P, 2, SEQ], R32)
        nk_lo = sb("nk_lo", [P, 2, SEQ], R32)
        cs = sb("cs", [P, 2, SEQ])
        t_sb = sb("t_sb", [P, SEQ])
        t_swap = sb("t_swap", [P, SEQ])
        t_rope = sb("t_rope", [P, SEQ])
        vn = sb("vn", [P, NT, 4, 2, HD], R32)
        prob = sb("prob", [P, 2, 1280])
        pt_hi = sb("pt_hi", [P, 3, 512], R32)
        pt_lo = sb("pt_lo", [P, 3, 512], R32)
        sz = sb("sz", [P, 2, SEQ])
        kon = sb("kon", [P, K_END])
        ident_r = sb("ident_r", [P, P], R32)
        mask_r = sb("mask_r", [P, P], R32)
        sel_r = sb("sel_r", [P, 8], R32)
        cum_r = sb("cum_r", [P, SEQ], R32)
        vecs = sb("vecs", [R_END, P])
        vecsT = sb("vecsT", [P, R_END])
        mod = sb("mod", [P, 16])
        amul = sb("amul", [P, KD])
        silc = sb("silc", [P, 2, KD])
        ssq = sb("ssq", [P, 8])
        rstd = sb("rstd", [P, 8])
        mhalf = sb("mhalf", [P, 4])
        bf = sb("bf", [8, 1])
        gates = sb("gates", [P, NT, 24])
        negm = sb("negm", [P, 2, 4])
        psum_row = sb("psum_row", [P, 2, 4])
        rinv = sb("rinv", [P, 2, 4])
        gg = sb("gg", [P, DM])
        w2k = sb("w2k", [P, 2, HD])
        w2v = sb("w2v", [P, HD])
        hid = sb("hid", [P, 2, NC])
        kcb_hi = sb("kcb_hi", [P, 2 * NC], R32)
        kcb_lo = sb("kcb_lo", [P, 2 * NC], R32)
        vcb = sb("vcb", [2 * NC, 2, HD], R32)
        pc = sb("pc", [P, NT, 2, NC])
        pcs = sb("pcs", [P, 3, NT * 2])
        pcT = sb("pcT", [2 * NC, 2, SEQ], R32)
        ybot = sb("ybot", [P, SEQ])
        ones = sb("ones", [P, P])
        with ExitStack() as early:
            x_sb = sb("x_sb", [P, NT, DM], F32, early)
        with ExitStack() as mid:
            qk_hi = sb("qk_hi", [P, 2, 2, SEQ], R32, mid)
            qk_lo = sb("qk_lo", [P, 2, 2, SEQ], R32, mid)
        with ExitStack() as late:
            x_res = sb("x_res", [P, NT, DM], F32, late)
        ctx.enter_context(nc.sbuf_tensor("hold", [P, NT, DM], F32))
        with ExitStack() as ffs:
            fz = sb("ff_z", [8, SEQ], F32, ffs)
            fe = sb("ff_e", [8, SEQ], F32, ffs)
            fc = sb("ff_c", [8, SEQ], F32, ffs)
            fo = sb("ff_o", [8, SEQ], F32, ffs)
            diag = sb("diag", [32, 4, 32], F32, ffs)
            asum = sb("asum", [P, 2, P], F32, ffs)
            ngt = sb("ngt", [32, SEQ], F32, ffs)
        y32 = sb("y32", [P, KD, SEQ])
        vf = sb("vf", [P, NT, FOX_H, 2, HD], R32)
        with ExitStack() as ada:
            side_raw = sb("side_raw", [P, 2, KD, P], F32, ada)
        with ExitStack() as cmp:
            U = sb("U", [P, 2, SEQ], F32, cmp)
            B = sb("B", [P, KC, 2, NCMP], F32, cmp)
        gsum = sb("gsum", [P, NSUM, P])

        raw_landed = [sem(f"raw_landed{i}") for i in range(NRAW)]
        raw_used, hi_done, split_done, wo_used = (sem(n) for n in ("raw_used", "hi_done", "split_done", "wo_used"))
        gate_prod, gate_sum = sem("gate_prod"), sem("gate_sum")
        x_in = [sem(f"x_in{i}") for i in range(NT)]
        xres_in, rows_in, cols_in, kon_in, rope_in, small_in = (sem(n) for n in (
            "xres_in", "rows_in", "cols_in", "kon_in", "rope_in", "small_in"))
        sq_done, var_done, rstd_done, xn_done = (sem(n) for n in ("sq_done", "var_done", "rstd_done", "xn_done"))
        consts_done, fills_done = sem("consts_done"), sem("fills_done")
        tanhc_done, silc_done, mod_done = (sem(n) for n in ("tanhc_done", "silc_done", "mod_done"))
        pj_ready, pj_act, pj_dve = sem("pj_ready"), sem("pj_act"), sem("pj_dve")
        ff_abs, ff_ln, ff_cum, ff_hi, ff_lo, ff_e = (sem(n) for n in (
            "ff_abs", "ff_ln", "ff_cum", "ff_hi", "ff_lo", "ff_e"))
        side_landed = [sem(f"side_landed{i}") for i in range(2)]
        ada_prod, ada_sum = sem("ada_prod"), sem("ada_sum")
        xT_ready, h_full, h_cut = sem("xT_ready"), sem("h_full"), sem("h_cut")
        t_swapped, rope_done = sem("t_swapped"), sem("rope_done")
        u_moved, b_done = sem("u_moved"), sem("b_done")
        s_ready, max_done, exp_done, p_ready = (sem(n) for n in ("s_ready", "max_done", "exp_done", "p_ready"))
        pt_ready, pt_hi_done, pt_lo_done, pv_done = (sem(n) for n in ("pt_ready", "pt_hi_done", "pt_lo_done", "pv_done"))
        y_ready, ybot_done, y_done, y_final = (sem(n) for n in ("y_ready", "ybot_done", "y_done", "y_final"))
        c_shift, c_exp, c_prob = sem("c_shift"), sem("c_exp"), sem("c_prob")
        yh_done, yl_done = sem("yh_done"), sem("yl_done")
        o_ready, osq_done, omul_done, ovar_done, orstd_done, o_done, stored = (sem(n) for n in (
            "o_ready", "osq_done", "omul_done", "ovar_done", "orstd_done", "o_done", "stored"))
        dve_own, pool_own = sem("dve_own"), sem("pool_own")

        ident = kon[:, K_ID:K_ID + P]

        def h_scratch(d):
            t = H_ORDER.index(d)
            return prob[:, t % 2, 512 * (t // 2 % 2):512 * (t // 2 % 2) + 512]

        block = ctx.enter_context(nc.Block())

        @block.sync
        def _(sp):
            w_in_k = w_in.rearrange("(k p) n -> p k n", p=P)
            w_ada_k = w_ada.rearrange("(k p) n -> p k n", p=P)
            first_col = dict(vs=C_VS, vw=C_VW, kc=C_KC, vc=C_VC, ks=C_KS, kw=C_KW)
            tile_col = dict(fv=C_FV, fq=C_FQ, fk=C_FK, fz=C_FZ)

            def pieces(kind, i, dst):
                if kind == "ada":
                    return [(dst, w_ada_k[:, :, i * P:(i + 1) * P])]
                if kind == "gate":
                    return [(dst, w_ada_k[:, :, 2 * DM + i * P:2 * DM + (i + 1) * P])]
                if kind in ("hidk", "hidv"):
                    w1 = (w_cmp_k1 if kind == "hidk" else w_cmp_v1).rearrange("(k p) n -> p k n", p=P)
                    return [(dst, w1[:, 8 * i:8 * i + 8, :])]
                if kind == "ffng":
                    return [(dst[:, :, 0:8], w_in_k[:, :, C_FF:C_FF + 8]),
                            (dst[:, :, 8:32], w_in_k[:, :, C_NG:C_NG + 24])]
                if kind in ("nq", "nz"):
                    c0 = (C_NQ if kind == "nq" else C_NZ) + i * HD
                    return [(dst[:, :, 0:HD], w_in_k[:, :, c0:c0 + HD]),
                            (dst[:, :, HD:P], w_in_k[:, :, c0 + 4 * HD:c0 + 5 * HD])]
                if kind == "wo":
                    pair = ORDER[i]
                    if pair < KD // 2:
                        return [(dst.rearrange("p k n -> p (k n)"), w_out[pair * P:(pair + 1) * P, :])]
                    r0 = FOX_W + (pair - KD // 2) * HD
                    return [(dst[0:HD].rearrange("p k n -> p (k n)"), w_out[r0:r0 + HD, :]),
                            (dst[HD:P].rearrange("p k n -> p (k n)"), w_out[r0 + 4 * HD:r0 + 5 * HD, :])]
                c0 = first_col[kind] if kind in first_col else tile_col[kind] + i * P
                return [(dst, w_in_k[:, :, c0:c0 + P])]

            sp.dma_start(vecsT[:, :], vec_cols).then_inc(cols_in, 16)
            for n, (kind, i) in enumerate(UNITS):
                if n >= NRAW:
                    before = UNITS[n - NRAW]
                    if before in MIDJOB:
                        sp.wait_ge(raw_used, MIDJOB.index(before) + 1)
                    elif before[0] in DIRECT:
                        sp.wait_ge(pj_ready, JOB_OF[before] + 1)
                    elif before[0] == "gate":
                        sp.wait_ge(gate_sum, before[1] + 1)
                    else:
                        sp.wait_ge(split_done, SPLITN[before] + 1)
                for dst, src in pieces(kind, i, raw[:, n % NRAW, :, :]):
                    sp.dma_start(dst, src).then_inc(raw_landed[n % NRAW], 16)
                if n < NT:
                    sp.dma_start(x_sb[:, n, :], x[n * P:(n + 1) * P, :]).then_inc(x_in[n], 16)
                if kind == "ada" and i in SIDE_BEHIND:
                    t = SIDE_BEHIND.index(i)
                    if t >= 2:
                        sp.wait_ge(ada_sum, t - 1)
                    for dst, src in pieces("ada", SIDE[t], side_raw[:, t % 2, :, :]):
                        sp.dma_start(dst, src).then_inc(side_landed[t % 2], 16)
            sp.wait_ge(s_ready, 3 * NI)
            for m in range(NT):
                sp.dma_start(x_res[:, m, :], x[m * P:(m + 1) * P, :]).then_inc(xres_in, 16)
            for m in range(NT):
                if m < NT - 1:
                    sp.wait_ge(o_done, 2 * (m + 1))
                    sp.dma_start(out[m * P:(m + 1) * P, :], x_res[:, m, :]).then_inc(stored, 16)
                    continue
                for half in range(2):
                    cols = slice(512 * half, 512 * half + 512)
                    sp.wait_ge(o_done, 2 * m + half + 1)
                    sp.dma_start(out[m * P:(m + 1) * P, cols], x_res[:, m, cols]).then_inc(stored, 16)
            sp.wait_ge(stored, 16 * (NT + 1))

        @block.gpsimd
        def _(pool):
            own = [0]

            def link(ins):
                own[0] += 1
                ins.then_inc(pool_own, 1)
                pool.wait_ge(pool_own, own[0])

            def row_roots():
                pool.wait_ge(fills_done, 1)
                pool.wait_ge(var_done, 1)
                pool.tensor_tensor(rstd[:, 0:NT], ssq[:, 0:NT], mhalf[:, 0:NT], ALU.pow).then_inc(rstd_done, 1)

            pool.memset(mhalf[:, :], -0.5).then_inc(fills_done, 1)
            pool.memset(kcb_hi[:, :].bitcast(F32), 0.0).then_inc(fills_done, 1)
            pool.memset(kcb_lo[:, :].bitcast(F32), 0.0).then_inc(fills_done, 1)
            pool.memset(ones[:, :], 1.0).then_inc(fills_done, 1)
            pool.memset(hid[:, :, :], 0.0).then_inc(fills_done, 1)
            pool.memset(cum_r[:, :].bitcast(F32), 0.0).then_inc(fills_done, 1)
            pool.memset(fo[:, :], 1.0).then_inc(fills_done, 1)
            pool.wait_ge(silc_done, 1)
            for t in range(len(SIDE)):
                if t == ROOTS_BEFORE:
                    row_roots()
                pool.wait_ge(side_landed[t % 2], 16 * (t // 2 + 1))
                src = side_raw[:, t % 2, :, :]
                pool.tensor_tensor(src, src, silc[:, 0, :].unsqueeze(2).to_broadcast([P, KD, P]), ALU.mult)\
                    .then_inc(ada_prod, 1)

            def prepare(u):
                src = raw[:, UNIT[u] % NRAW, :, :]
                if u[0] == "gate":
                    pool.wait_ge(raw_landed[UNIT[u] % NRAW], landed(UNIT[u]))
                    pool.tensor_tensor(src, src, silc[:, 0, :].unsqueeze(2).to_broadcast([P, KD, P]), ALU.mult)\
                        .then_inc(gate_prod, 1)
                    return
                n = SPLITN[u]
                w = 32 if u[0] == "ffng" else P
                pool.wait_ge(hi_done, n + 1)
                pool.tensor_tensor(w_lo[:, n % NSPLIT, :, 0:w], src[:, :, 0:w],
                                   w_hi[:, n % NSPLIT, :, 0:w].bitcast(F32), ALU.subtract).then_inc(split_done, 1)

            def rope_rest(job):
                n = ROPEN[job]
                kind, i = job
                pool.wait_ge(t_swapped, 64 * (n + 1))
                pool.wait_ge(pj_dve, emptied("D", JOB[job]))
                link(pool.tensor_tensor(t_swap[:, :], t_swap[:, :], cs[:, 1, :], ALU.mult))
                if kind == "kc":
                    pool.tensor_tensor(t_rope[:, :], t_rope[:, :], t_swap[:, :], ALU.add).then_inc(rope_done, 1)
                    return
                link(pool.tensor_tensor(t_rope[:, :], t_rope[:, :], t_swap[:, :], ALU.add))
                if kind == "nq":
                    k = PLACE[4 + i]
                    if k >= 2:
                        pool.wait_ge(s_ready, 3 * (LAST_STEP[k - 2] + 1))
                    hi, lo = qk_hi[:, k % 2, 0, :], qk_lo[:, k % 2, 0, :]
                else:
                    b = 0 if kind == "ks" else 1
                    hi, lo = nk_hi[:, b, :], nk_lo[:, b, :]
                link(pool.tensor_copy(hi, t_rope[:, :]))
                pool.tensor_tensor(lo, t_rope[:, :], hi.bitcast(F32), ALU.subtract).then_inc(rope_done, 1)

            def blocks(which):
                row = R_PEK if which == 0 else R_PEV
                pool.wait_ge(u_moved, 64 * (which + 1))
                if which:
                    pool.wait_ge(pj_ready, JOB["hidk", 0] + 1)
                for g in range(2):
                    src = bass.AP(tensor=U, offset=g * SEQ,
                                  ap=[[2 * SEQ, P], [2, KC], [CMP_STRIDE, NCMP]])
                    pe = vecsT[:, row:row + KC].unsqueeze(2).to_broadcast([P, KC, NCMP])
                    pool.tensor_tensor(B[:, :, g, :], src, pe, ALU.add).then_inc(b_done, 1)

            pool.wait_ge(cols_in, 16)
            pool.wait_ge(rope_in, 16)
            pool.wait_ge(silc_done, 1)
            def behind(j):
                for u in POOL_AFTER[j]:
                    if u[0] == "rope":
                        rope_rest(u[1])
                    else:
                        prepare(u)
                if j == ("ks", 0):
                    blocks(0)
                if j == ("hidk", 0):
                    blocks(1)

            def y_gate(k):
                p = ORDER[k]
                pool.wait_ge(y_done, 2 * k + 2)
                pool.wait_ge(pj_dve, emptied("D", JOB[("fz", p) if p < 4 else ("nz", p - 4)]))
                pool.tensor_tensor(y32[:, p, :], y32[:, p, :], sz[:, k % 2, :], ALU.mult).then_inc(y_final, 1)

            for j in PROLOGUE:
                behind(j)
            for s in range(NI + 2):
                if s - 2 in LAST_STEP:
                    y_gate(LAST_STEP.index(s - 2))
                for j in FILL[s] if s < NI else []:
                    behind(j)
            for u in PREP_LAST:
                prepare(u)
            for m in range(NT):
                pool.wait_ge(ovar_done, m + 1)
                pool.tensor_tensor(rstd[:, m:m + 1], ssq[:, 2 * m:2 * m + 1], mhalf[:, 0:1], ALU.pow)\
                    .then_inc(orstd_done, 1)

        @block.scalar
        def _(act):
            act.dma_start(kon[:, :], consts).then_inc(kon_in, 16)
            act.wait_ge(cols_in, 16)
            act.activation(silc[:, 1, :], vecsT[:, R_C:R_C + KD], ACT.Tanh, scale=0.5).then_inc(tanhc_done, 1)
            act.dma_start(cs[:, :, :], rope).then_inc(rope_in, 16)
            act.dma_start(bf[:, :], b_forget.rearrange("o h -> h o")).then_inc(small_in, 16)
            act.dma_start(w2k[:, 0, :], w_cmp_k2).then_inc(small_in, 16)
            act.dma_start(w2k[:, 1, :], w_cmp_k2).then_inc(small_in, 16)
            act.dma_start(w2v[:, :], w_cmp_v2).then_inc(small_in, 16)
            act.dma_start(vecs[:, :], vec_rows).then_inc(rows_in, 16)
            for m in range(NT):
                act.wait_ge(x_in[m], 16)
                if m:
                    act.wait_ge(sq_done, m)
                act.activation(prob[:, 0, 0:DM], x_sb[:, m, :], ACT.Square,
                               accum_out=ssq[:, m:m + 1]).then_inc(sq_done, 1)

            def move_u(which, src):
                for g in range(2):
                    rows = src[g * HD:(g + 1) * HD, :]
                    act.dma_start(U[0:HD, g, :], rows).then_inc(u_moved, 16)
                    act.dma_start(U[HD:P, g, 0:SEQ - 1], rows[:, 1:SEQ]).then_inc(u_moved, 16)

            def h_of(d, src, done):
                act.wait_ge(mod_done, 1)
                t = H_ORDER.index(d)
                if t >= 4:
                    act.wait_ge(h_cut, t - 3)
                act.activation(h_scratch(d), src[:, :], ACT.Identity, bias=mod[:, d:d + 1],
                               scale=amul[:, d:d + 1]).then_inc(done, 1)

            act.wait_ge(sq_done, NT)
            t_jobs = [j for j in JOBS if j[0] in ("kc", "ks", "kw", "nq", "vc")]

            def evac(job):
                n = JOB[job]
                kind, i = job
                src = PJ_BANK[n % 2]
                if "A" not in READERS[kind]:
                    return
                act.wait_ge(pj_ready, n + 1)
                if kind == "xT":
                    h_of(i, src, pj_act)
                elif kind == "vsw":
                    act.activation(vn[:, 2 * i:2 * i + 2, :, 0, :], src[:, :].rearrange("p (m h d) -> p m h d", m=2, h=4),
                                   ACT.Copy).then_inc(pj_act, 1)
                elif kind == "fv":
                    half, m2 = i // 2, i % 2
                    act.activation(vf[:, 2 * m2:2 * m2 + 2, 4 * half:4 * half + 4, 0, :],
                                   src[:, :].rearrange("p (m h d) -> p m h d", m=2, h=4), ACT.Copy).then_inc(pj_act, 1)
                elif kind in ("fq", "fk"):
                    k = PLACE[i]
                    if k >= 2:
                        act.wait_ge(s_ready, 3 * (LAST_STEP[k - 2] + 1))
                    w = 0 if kind == "fq" else 1
                    act.activation(qk_hi[:, k % 2, w, :], src[:, :], ACT.Copy,
                                   scale=QSCALE if w == 0 else 1.0).then_inc(pj_act, 1)
                elif kind == "ffng":
                    act.activation(ngt[:, :], src[0:32, :], ACT.Tanh, scale=0.5).then_inc(pj_act, 1)
                elif kind in ("kc", "ks", "kw", "nq", "vc"):
                    k = t_jobs.index(job)
                    before = t_jobs[:k]
                    if before:
                        act.wait_ge(t_swapped, 64 * sum(j[0] != "vc" for j in before))
                        if ("vc", 0) in before:
                            act.wait_ge(u_moved, 128)
                    act.activation(t_sb[:, :], src[:, :], ACT.Copy,
                                   scale=QSCALE if kind == "nq" else 1.0)\
                       .then_inc(pj_act, 1)
                    act.wait_ge(pj_act, emptied("A", n))
                    if kind == "vc":
                        act.wait_ge(b_done, 2)
                        move_u(1, t_sb)
                    else:
                        r = ROPEN[job]
                        if r:
                            act.wait_ge(rope_done, r)
                        for q in range(4):
                            act.dma_start(t_swap[32 * q:32 * q + 32, :],
                                          t_sb[32 * (q ^ 1):32 * (q ^ 1) + 32, :]).then_inc(t_swapped, 16)
                elif kind in ("fz", "nz"):
                    k = PLACE[i if kind == "fz" else 4 + i]
                    if k >= 2:
                        act.wait_ge(y_final, k - 1)
                    act.activation(sz[:, k % 2, :], src[:, :], ACT.Tanh, scale=0.5).then_inc(pj_act, 1)
                elif kind in ("hidk", "hidv"):
                    act.wait_ge(fills_done, 7)
                    if kind == "hidv":
                        act.wait_ge(pj_ready, JOB["kc2", 0] + 1)
                    act.activation(hid[:, :, 0:NCMP], src[:, 0:2 * NCMP].rearrange("p (g n) -> p g n", g=2),
                                   ACT.Tanh, scale=0.5).then_inc(pj_act, 1)
                elif kind == "kc2":
                    act.wait_ge(fills_done, 7)
                    act.activation(kcb_hi[0:HD, 0:NC], src[0:HD, 0:NC], ACT.Copy, scale=0.5)
                    act.activation(kcb_hi[HD:P, NC:2 * NC], src[HD:P, NC:2 * NC], ACT.Copy, scale=0.5)\
                       .then_inc(pj_act, 1)
                elif kind == "vc2":
                    act.activation(vcb[:, 0, :], src[0:2 * NC, 0:HD], ACT.Copy, scale=0.5).then_inc(pj_act, 1)
                elif kind == "PcT":
                    if i:
                        act.wait_ge(y_ready, 2 * i)
                    act.activation(pcT[:, 0, :], src[0:2 * NC, :], ACT.Copy).then_inc(pj_act, 1)
                elif kind == "gate":
                    act.activation(gg[:, 2 * i * P:2 * (i + 1) * P], src[:, 2 * P:4 * P], ACT.Copy).then_inc(pj_act, 1)

            def after(job):
                kind, i = job
                if kind == "kc":
                    act.wait_ge(rope_done, 1)
                    move_u(0, t_rope)
                if kind == "ffng":
                    act.wait_ge(ff_abs, 1)
                    act.activation(fe[:, :], fe[:, :], ACT.Exp, scale=-1.0).then_inc(ff_e, 1)
                    act.wait_ge(ff_e, 1)
                    act.activation(fe[:, :], fe[:, :], ACT.Ln, bias=1.0).then_inc(ff_ln, 1)
                if kind == "Sc":
                    act.wait_ge(c_shift, i + 1)
                    act.activation(pc[:, :, :, :], pc[:, :, :, :], ACT.Exp).then_inc(c_exp, 1)

            for j in PROLOGUE:
                evac(j)
                if j == ("xT", KD - 1):
                    for d in range(EARLY_X):
                        act.wait_ge(xT_ready, d + 1)
                        h_of(d, bank[d], h_full)
                if j[0] == "ffng":
                    after(j)
                if j == ("vsw", 1):
                    act.wait_ge(ff_cum, 1)
                    act.activation(cum_r[0:8, :], fc[:, :], ACT.Copy, scale=-1.0).then_inc(ff_hi, 1)
                if j == ("fv", 1):
                    after(("kc", 0))

            def exps(s):
                for k, (q, g, col, n) in enumerate(QT):
                    if col == 0:
                        act.wait_ge(max_done, 3 * s + g + 1)
                    if k == 0 and s >= 2:
                        act.wait_ge(pt_ready, 3 * (s - 2) + 3)
                    if k == 0 and s >= 2:
                        act.wait_ge(p_ready, s - 1)
                    last = act.activation(prob[:, s % 2, POFF[q]:POFF[q] + n], S_BANK[g][:, col:col + n], ACT.Exp,
                                          bias=negm[:, s % 2, q:q + 1], scale=1.0,
                                          accum_out=psum_row[:, s % 2, q:q + 1])
                    if k != 1:
                        last.then_inc(exp_done, 1)

            def pt_copy(s, j):
                n = 3 * s + j
                act.wait_ge(pt_ready, n + 1)
                if n >= 3:
                    act.wait_ge(pv_done, n - 2)
                act.activation(pt_hi[:, j, 0:PTW[j]], PT_BANK[n % 2][:, 0:PTW[j]], ACT.Copy).then_inc(pt_hi_done, 1)

            def y_bottom(s):
                _, a, b = INST[s]
                h = head_of(s)
                if b is None:
                    act.wait_ge(pv_done, 3 * s + 3)
                else:
                    act.wait_ge(y_ready, h - FOX_H + 1)
                act.activation(ybot[HD * a:HD * a + HD, :], Y_BANK[HD:P, :], ACT.Copy).then_inc(ybot_done, 1)

            def y_high(k):
                t = ORDER[k]
                act.wait_ge(pj_ready, LAST_H + 1)
                act.wait_ge(y_final, k + 1)
                act.activation(hT_hi[:, t, :], y32[:, t, :], ACT.Copy, scale=0.5).then_inc(yh_done, 1)

            for s in range(NI + 2):
                if 1 <= s <= NI:
                    pt_copy(s - 1, 0)
                    pt_copy(s - 1, 1)
                if s < NI:
                    exps(s)
                if 1 <= s <= NI:
                    pt_copy(s - 1, 2)
                if s >= 2 and last_of_head(s - 2):
                    y_bottom(s - 2)
                for j in FILL[s] if s < NI else []:
                    evac(j)
                    if j[0] == "Sc":
                        after(j)
                for k in Y_SPLIT.get(s, ()):
                    y_high(k)
            for m in range(NT):
                for half in range(2):
                    act.wait_ge(o_ready, 2 * m + half + 1)
                    act.wait_ge(yl_done, KD)
                    act.activation(y32[:, 2 * m + half, :], bank[2 * m + half][:, :], ACT.Square,
                                   accum_out=ssq[:, 2 * m + half:2 * m + half + 1]).then_inc(osq_done, 1)

        @block.vector
        def _(dve):
            own = [0]

            def link(ins):
                own[0] += 1
                ins.then_inc(dve_own, 1)
                dve.wait_ge(dve_own, own[0])

            dve.wait_ge(cols_in, 16)
            dve.wait_ge(tanhc_done, 1)
            link(dve.scalar_tensor_tensor(silc[:, 0, :], silc[:, 1, :], 1.0, vecsT[:, R_C:R_C + KD],
                                          ALU.add, ALU.mult))
            dve.tensor_scalar(silc[:, 0, :], silc[:, 0, :], 0.5, None, ALU.mult).then_inc(silc_done, 1)
            dve.wait_ge(kon_in, 16)
            dve.tensor_copy(ident_r[:, :], ident).then_inc(consts_done, 1)
            dve.tensor_copy(mask_r[:, :], kon[:, K_MASK:K_MASK + P]).then_inc(consts_done, 1)
            dve.tensor_copy(sel_r[:, :], kon[:, K_SEL:K_SEL + 8]).then_inc(consts_done, 1)

            def evac(job):
                n = JOB[job]
                kind, i = job
                src = PJ_BANK[n % 2]
                if "D" not in READERS[kind]:
                    return
                dve.wait_ge(pj_ready, n + 1)
                if "A" in READERS[kind]:
                    dve.wait_ge(pj_act, emptied("A", n))

                def low(dst, hi, frm, scale=1.0):
                    dve.scalar_tensor_tensor(dst, frm, scale, hi.bitcast(F32), ALU.mult, ALU.subtract)\
                       .then_inc(pj_dve, 1)

                if kind == "ada" and i in SIDE:
                    dve.tensor_copy(mod[:, i:i + 1], src[:, 0:1]).then_inc(pj_dve, 1)
                    if n == 15:
                        modulation()
                elif kind == "ada":
                    if i:
                        dve.wait_ge(pj_dve, emptied("D", n - 1))
                    for b in range(4):
                        last = dve.scalar_tensor_tensor(diag[:, b, :], src[0:32, 32 * b:32 * b + 32], 1.0,
                                                        kon[0:32, K_ID:K_ID + 32], ALU.mult, ALU.mult,
                                                        accum_out=mod[32 * b:32 * b + 32, i:i + 1])
                    last.then_inc(pj_dve, 1)
                elif kind == "vsw":
                    v = vn[:, 2 * i:2 * i + 2, :, :, :]
                    dve.tensor_tensor(v[:, :, :, 1, :], src[:, :].rearrange("p (m h d) -> p m h d", m=2, h=4),
                                      v[:, :, :, 0, :].bitcast(F32), ALU.subtract).then_inc(pj_dve, 1)
                elif kind == "fv":
                    half, m2 = i // 2, i % 2
                    v = vf[:, 2 * m2:2 * m2 + 2, 4 * half:4 * half + 4, :, :]
                    dve.tensor_tensor(v[:, :, :, 1, :], src[:, :].rearrange("p (m h d) -> p m h d", m=2, h=4),
                                      v[:, :, :, 0, :].bitcast(F32), ALU.subtract).then_inc(pj_dve, 1)
                elif kind in ("fq", "fk"):
                    w = 0 if kind == "fq" else 1
                    k = PLACE[i]
                    low(qk_lo[:, k % 2, w, :], qk_hi[:, k % 2, w, :], src[:, :], QSCALE if w == 0 else 1.0)
                elif kind == "ffng":
                    forget(src)
                elif kind in ("kc", "ks", "kw", "nq"):
                    r = ROPEN[job]
                    dve.wait_ge(rope_in, 16)
                    if r:
                        dve.wait_ge(rope_done, r)
                    if r == 1:
                        dve.wait_ge(u_moved, 64)
                    dve.scalar_tensor_tensor(t_rope[:, :], src[:, :], QSCALE if kind == "nq" else 1.0, cs[:, 0, :],
                                             ALU.mult, ALU.mult).then_inc(pj_dve, 1)
                elif kind == "ngT":
                    dve.tensor_scalar(gates[:, :, :], src[:, 0:NT * 32].rearrange("p (m n) -> p m n", m=NT)[:, :, 8:32],
                                      1.0, 0.5, ALU.add, ALU.mult).then_inc(pj_dve, 1)
                elif kind in ("fz", "nz"):
                    k = PLACE[i if kind == "fz" else 4 + i]
                    dve.scalar_tensor_tensor(sz[:, k % 2, :], sz[:, k % 2, :], 1.0, src[:, :], ALU.add, ALU.mult)\
                       .then_inc(pj_dve, 1)
                elif kind in ("hidk", "hidv"):
                    dve.scalar_tensor_tensor(hid[:, :, 0:NCMP], hid[:, :, 0:NCMP], 1.0,
                                             src[:, 0:2 * NCMP].rearrange("p (g n) -> p g n", g=2),
                                             ALU.add, ALU.mult).then_inc(pj_dve, 1)
                elif kind == "kc2":
                    dve.scalar_tensor_tensor(kcb_lo[0:HD, 0:NC], src[0:HD, 0:NC], 0.5,
                                             kcb_hi[0:HD, 0:NC].bitcast(F32), ALU.mult, ALU.subtract)
                    dve.scalar_tensor_tensor(kcb_lo[HD:P, NC:2 * NC], src[HD:P, NC:2 * NC], 0.5,
                                             kcb_hi[HD:P, NC:2 * NC].bitcast(F32), ALU.mult, ALU.subtract)\
                       .then_inc(pj_dve, 1)
                elif kind == "vc2":
                    low(vcb[:, 1, :], vcb[:, 0, :], src[0:2 * NC, 0:HD], 0.5)
                elif kind == "PcT":
                    low(pcT[:, 1, :], pcT[:, 0, :], src[0:2 * NC, :])
                elif kind == "Sc":
                    compressed(i, src)
                elif kind == "gate":
                    cols = slice(2 * i * P, 2 * (i + 1) * P)
                    dve.tensor_tensor(gg[:, cols], src[:, 0:2 * P], gg[:, cols], ALU.mult).then_inc(pj_dve, 1)

            def side_sum(t):
                dve.wait_ge(ada_prod, t + 1)
                if t >= 2:
                    dve.wait_ge(pj_ready, JOB["ada", SIDE[t - 2]] + 1)
                dve.tensor_reduce(asum[:, t % 2, :], side_raw[:, t % 2, :, :].rearrange("p k n -> p n k"), AX_X, ALU.add)\
                   .then_inc(ada_sum, 1)

            def modulation():
                dve.wait_ge(pj_dve, emptied("D", len(ADA_ORDER) - 1))
                link(dve.tensor_tensor(mod[:, :], mod[:, :], vecsT[:, R_ADA:R_ADA + 16], ALU.add))
                dve.scalar_tensor_tensor(amul[:, :], mod[:, 8:16], 1.0, vecsT[:, R_GPRE:R_GPRE + 8],
                                         ALU.add, ALU.mult).then_inc(mod_done, 1)

            def forget(src):
                dve.wait_ge(small_in, 64)
                dve.wait_ge(fills_done, 7)
                dve.tensor_scalar(fz[:, :], src[0:8, :], bf[:, 0:1], None, ALU.add).then_inc(pj_dve, 1)
                dve.wait_ge(pj_dve, emptied("D", JOB["ffng", 0]))
                dve.scalar_tensor_tensor(fe[:, :], fz[:, :], -1.0, fz[:, :], ALU.mult, ALU.max).then_inc(ff_abs, 1)

            def forget_sum():
                dve.wait_ge(ff_ln, 1)
                link(dve.scalar_tensor_tensor(fz[:, :], fz[:, :], 0.0, fe[:, :], ALU.min, ALU.subtract))
                dve.tensor_tensor_scan(fc[:, :], fo[:, :], fz[:, :], 0.0, ALU.mult, ALU.add).then_inc(ff_cum, 1)

            def compressed(i, src):
                s3 = src[:, 0:NT * 2 * NC].rearrange("p (m a n) -> p m a n", m=NT, a=2)
                rows = pcs[:, 0, :].rearrange("p (m a) -> p m a", m=NT)
                cmask = kon[:, K_CMASK:K_CMASK + NT * NC].rearrange("p (m n) -> p m n", m=NT)
                if i:
                    dve.wait_ge(pj_ready, JOB["PcT", i - 1] + 1)
                last = [dve.tensor_tensor(pc[:, :, a, :], s3[:, :, a, :], cmask, ALU.add) for a in range(2)][-1]
                last.then_inc(pj_dve, 1)
                dve.wait_ge(pj_dve, emptied("D", JOB["Sc", i]))
                link(dve.tensor_reduce(rows, pc[:, :, :, :], AX_X, ALU.max))
                link(dve.tensor_scalar(rows, rows, NEG / 10, None, ALU.max))
                flat = pc[:, :, :, :].rearrange("p m a n -> p (m a) n")
                dve.tensor_tensor(flat, flat, pcs[:, 0, :].unsqueeze(2).to_broadcast([P, 2 * NT, NC]),
                                  ALU.subtract).then_inc(c_shift, 1)
                dve.wait_ge(c_exp, i + 1)
                link(dve.tensor_reduce(pcs[:, 1, :].rearrange("p (m a) -> p m a", m=NT), pc[:, :, :, :], AX_X, ALU.add))
                link(dve.tensor_scalar(pcs[:, 1, :], pcs[:, 1, :], 1e-30, None, ALU.max))
                link(dve.reciprocal(pcs[:, 2, :], pcs[:, 1, :]))
                g = bass.AP(tensor=gates, offset=3 * i, ap=[[NT * 24, P], [24, NT], [12, 2]])
                r = pcs[:, 2, :].rearrange("p (m a) -> p m a", m=NT)
                link(dve.tensor_tensor(r, r, g, ALU.mult))
                dve.tensor_tensor(flat, flat, pcs[:, 2, :].unsqueeze(2).to_broadcast([P, 2 * NT, NC]),
                                  ALU.mult).then_inc(c_prob, 1)

            def prepare(u):
                slot = UNIT[u] % NRAW
                if u[0] == "gate":
                    dve.wait_ge(gate_prod, u[1] + 1)
                    if u[1] >= NSUM:
                        dve.wait_ge(pj_ready, JOB["gate", (u[1] - NSUM) // 2] + 1)
                    dve.tensor_reduce(gsum[:, u[1] % NSUM, :], raw[:, slot, :, :].rearrange("p k n -> p n k"), AX_X, ALU.add)\
                       .then_inc(gate_sum, 1)
                    return
                n = SPLITN[u]
                w = 32 if u[0] == "ffng" else P
                dve.wait_ge(raw_landed[slot], landed(UNIT[u]))
                if n >= NSPLIT:
                    before = SPLIT[n - NSPLIT]
                    if before[0] == "wo":
                        dve.wait_ge(wo_used, before[1] + 1)
                    else:
                        dve.wait_ge(pj_ready, JOB_OF[before] + 1)
                dve.tensor_copy(w_hi[:, n % NSPLIT, :, 0:w], raw[:, slot, :, 0:w]).then_inc(hi_done, 1)

            def cut_h(d):
                link(dve.tensor_copy(hT_hi[:, d, :], h_scratch(d)))
                dve.tensor_tensor(hT_lo[:, d, :], h_scratch(d), hT_hi[:, d, :].bitcast(F32), ALU.subtract)\
                   .then_inc(h_cut, 1)

            for j in PROLOGUE:
                for t, i in enumerate(SIDE):
                    if JOB["ada", i] == JOB[j] + 1:
                        side_sum(t)
                evac(j)
                if JOB[j] == MEAN_SQUARES_AT:
                    dve.wait_ge(sq_done, NT)
                    dve.tensor_scalar(ssq[:, 0:NT], ssq[:, 0:NT], 1.0 / DM, EPS, ALU.mult, ALU.add).then_inc(var_done, 1)
                if JOB[j] == SCALE_X_AT:
                    dve.wait_ge(rstd_done, 1)
                    for m in range(NT):
                        dve.tensor_scalar(x_sb[:, m, :], x_sb[:, m, :], rstd[:, m:m + 1], None, ALU.mult)\
                           .then_inc(xn_done, 1)
                if j[0] == "xT":
                    dve.wait_ge(pj_act, emptied("A", JOB[j]))
                    cut_h(j[1])
                if j == ("xT", KD - 1):
                    for d in range(EARLY_X):
                        dve.wait_ge(h_full, d + 1)
                        cut_h(d)
                if j == ("vsw", 0):
                    forget_sum()
                if j == ("vsw", 1):
                    dve.wait_ge(ff_hi, 1)
                    dve.scalar_tensor_tensor(cum_r[32:40, :], fc[:, :], -1.0, cum_r[0:8, :].bitcast(F32),
                                             ALU.mult, ALU.subtract).then_inc(ff_lo, 1)
                for u in PREP_AFTER[j] if j != PROLOGUE[-1] else []:
                    prepare(u)
            late = PREP_AFTER[PROLOGUE[-1]]

            def maxima(s):
                if s >= 2:
                    dve.wait_ge(exp_done, 3 * (s - 1))
                for k, (q, g, col, n) in enumerate(QT):
                    if col == 0:
                        dve.wait_ge(s_ready, 3 * s + g + 1)
                    last = dve.tensor_reduce(negm[:, s % 2, q:q + 1], S_BANK[g][:, col:col + n], AX_X, ALU.max,
                                             negate=True)
                    if k != 1:
                        last.then_inc(max_done, 1)

            def y_out(s):
                p, a, _ = INST[s]
                h = heads_before(s)
                r = slice(HD * a, HD * a + HD)
                dve.wait_ge(ybot_done, h + 1)
                dve.tensor_tensor(y32[r, p, :], Y_BANK[0:HD, :], ybot[r, :], ALU.add).then_inc(y_done, 1)

            def pt_low(s, j):
                n = 3 * s + j
                dve.wait_ge(pt_hi_done, n + 1)
                dve.tensor_tensor(pt_lo[:, j, 0:PTW[j]], PT_BANK[n % 2][:, 0:PTW[j]],
                                  pt_hi[:, j, 0:PTW[j]].bitcast(F32), ALU.subtract).then_inc(pt_lo_done, 1)

            def normalise(s):
                p, a, b = INST[s]
                dve.wait_ge(exp_done, 3 * s + 3)
                r = rinv[:, s % 2, :]
                link(dve.reciprocal(r, psum_row[:, s % 2, :]))
                if b is not None:
                    col = 3 * (p - 4 + 4 * a) + 1 + b
                    g = bass.AP(tensor=gates, offset=col, ap=[[NT * 24, P], [24, NT]])
                    link(dve.tensor_tensor(r, r, g, ALU.mult))
                for q, _, _, n in QT:
                    last = dve.tensor_scalar(prob[:, s % 2, POFF[q]:POFF[q] + n], prob[:, s % 2, POFF[q]:POFF[q] + n],
                                             rinv[:, s % 2, q:q + 1], None, ALU.mult)
                last.then_inc(p_ready, 1)

            def y_low(k):
                t = ORDER[k]
                dve.wait_ge(yh_done, k + 1)
                dve.scalar_tensor_tensor(hT_lo[:, t, :], y32[:, t, :], 0.5, hT_hi[:, t, :].bitcast(F32), ALU.mult,
                                         ALU.subtract).then_inc(yl_done, 1)

            dve.wait_ge(pj_dve, emptied("D", JOB["ngT", 0]))
            for s in range(NI + 2):
                if 1 <= s <= NI:
                    pt_low(s - 1, 0)
                    pt_low(s - 1, 1)
                if s < NI:
                    maxima(s)
                if s < NI:
                    normalise(s)
                if 1 <= s <= NI:
                    pt_low(s - 1, 2)
                if s >= 2 and last_of_head(s - 2):
                    y_out(s - 2)
                for u in late:
                    prepare(u)
                late = []
                for j in FILL[s] if s < NI else []:
                    evac(j)
                    if j == FILL[s][-1]:
                        late = PREP_AFTER[j]
                    else:
                        for u in PREP_AFTER[j]:
                            prepare(u)
                for k in Y_SPLIT.get(s, ()):
                    y_low(k)

            for u in PREP_LAST:
                prepare(u)
            for m in range(NT):
                for half in range(2):
                    cols = slice(512 * half, 512 * half + 512)
                    dve.wait_ge(osq_done, 2 * m + half + 1)
                    if m >= 2:
                        dve.wait_ge(o_done, 2 * (m - 1))
                    dve.tensor_tensor(prob[:, m % 2, cols], bank[2 * m + half][:, :], gg[:, cols], ALU.mult)\
                       .then_inc(omul_done, 1)
                link(dve.tensor_tensor(ssq[:, 2 * m:2 * m + 1], ssq[:, 2 * m:2 * m + 1], ssq[:, 2 * m + 1:2 * m + 2],
                                       ALU.add))
                dve.tensor_scalar(ssq[:, 2 * m:2 * m + 1], ssq[:, 2 * m:2 * m + 1], 1.0 / DM, EPS, ALU.mult, ALU.add)\
                   .then_inc(ovar_done, 1)
                dve.wait_ge(orstd_done, m + 1)
                dve.wait_ge(omul_done, 2 * m + 2)
                dve.wait_ge(xres_in, 16 * NT)
                for half in range(2):
                    cols = slice(512 * half, 512 * half + 512)
                    dve.scalar_tensor_tensor(x_res[:, m, cols], prob[:, m % 2, cols], rstd[:, m:m + 1],
                                             x_res[:, m, cols], ALU.mult, ALU.add).then_inc(o_done, 1)

        @block.tensor
        def _(pe):
            def mm3(dst, l_hi, l_lo, r_hi, r_lo, start, stop):
                pe.matmul(dst, l_hi, r_hi, start=start, stop=False)
                pe.matmul(dst, l_hi, r_lo, start=False, stop=False)
                return pe.matmul(dst, l_lo, r_hi, start=False, stop=stop)

            def wait_raw(u):
                pe.wait_ge(raw_landed[UNIT[u] % NRAW], landed(UNIT[u]))
                return UNIT[u] % NRAW

            def wait_split(u):
                pe.wait_ge(split_done, SPLITN[u] + 1)
                return SPLITN[u] % NSPLIT

            def x_transposes(d, dst):
                for m in range(NT):
                    last = pe.transpose(dst[:, m * P:(m + 1) * P], x_sb[:, m, d * P:(d + 1) * P], ident)
                return last

            def job(j):
                n = JOB[j]
                kind, i = j
                dst = PJ_BANK[n % 2]
                if n >= 2:
                    a, d = emptied("A", n - 2), emptied("D", n - 2)
                    if a:
                        pe.wait_ge(pj_act, a)
                    if d:
                        pe.wait_ge(pj_dve, d)
                if kind == "ada" and i in SIDE:
                    t = SIDE.index(i)
                    pe.wait_ge(fills_done, 7)
                    pe.wait_ge(ada_sum, t + 1)
                    pe.matmul(dst[:, 0:1], asum[:, t % 2, :], ones[:, 0:1], start=True, stop=True).then_inc(pj_ready, 1)
                elif kind == "ada":
                    pe.wait_ge(silc_done, 1)
                    slot = wait_raw(j)
                    for k in range(KD):
                        last = pe.matmul(dst[0:32, 0:P], silc[:, 0, k:k + 1].to_broadcast([P, 32]), raw[:, slot, k, :],
                                         start=(k == 0), stop=(k == KD - 1))
                    last.then_inc(pj_ready, 1)
                elif kind == "xT":
                    x_transposes(i, dst).then_inc(pj_ready, 1)
                elif kind in ("vsw", "fv"):
                    if kind == "vsw":
                        wait_split(("vs", 0))
                        slot = wait_split(("vw", 0)) - 1
                        m2 = i
                    else:
                        half, m2 = i // 2, i % 2
                        slot = wait_split(("fv", 2 * half + 1)) - 1
                    for m in range(2):
                        tok = slice((2 * m2 + m) * P, (2 * m2 + m + 1) * P)
                        for k in range(KD):
                            last = mm3(dst[:, 256 * m:256 * m + 256], hT_hi[:, k, tok], hT_lo[:, k, tok],
                                       w_hi[:, slot:slot + 2, k, :], w_lo[:, slot:slot + 2, k, :],
                                       k == 0, k == KD - 1)
                    last.then_inc(pj_ready, 1)
                elif kind == "ffng":
                    slot = wait_split(j)
                    for k in range(KD):
                        last = mm3(dst[0:32, :], w_hi[:, slot, k, 0:32], w_lo[:, slot, k, 0:32], hT_hi[:, k, :],
                                   hT_lo[:, k, :], k == 0, k == KD - 1)
                    last.then_inc(pj_ready, 1)
                elif kind == "ngT":
                    pe.wait_ge(pj_act, emptied("A", JOB["ffng", 0]))
                    for m in range(NT):
                        last = pe.transpose(dst[:, 32 * m:32 * m + 32], ngt[:, m * P:(m + 1) * P], ident[0:32, 0:32])
                    last.then_inc(pj_ready, 1)
                elif kind in ("kc", "fq", "fk", "fz", "vc", "ks", "nq", "kw", "nz"):
                    slot = wait_split(j)
                    for t, k in enumerate(H_ORDER):
                        if kind == "kc":
                            pe.wait_ge(h_cut, t + 1)
                        last = mm3(dst[:, :], w_hi[:, slot, k, :], w_lo[:, slot, k, :], hT_hi[:, k, :], hT_lo[:, k, :],
                                   t == 0, t == KD - 1)
                    last.then_inc(pj_ready, 1)
                elif kind in ("hidk", "hidv"):
                    pe.wait_ge(b_done, 2 if kind == "hidk" else 4)
                    for kk in range(KC):
                        if kk % 8 == 0:
                            slot = wait_raw((kind, kk // 8))
                        last = pe.matmul(dst[:, 0:2 * NCMP], raw[:, slot, kk % 8, :],
                                         B[:, kk, :, :].rearrange("p g n -> p (g n)"),
                                         start=(kk == 0), stop=(kk == KC - 1))
                        if kk == 7:
                            last.then_inc(raw_used, 1)
                    last.then_inc(pj_ready, 1)
                elif kind in ("kc2", "vc2"):
                    pe.wait_ge(small_in, 64)
                    pe.wait_ge(pj_dve, emptied("D", JOB["hidk" if kind == "kc2" else "hidv", 0]))
                    h2 = hid[:, :, :].rearrange("p g n -> p (g n)")
                    if kind == "kc2":
                        pe.matmul(dst[:, 0:2 * NC], w2k[:, :, :].rearrange("p a n -> p (a n)"), h2,
                                  start=True, stop=True).then_inc(pj_ready, 1)
                    else:
                        pe.matmul(dst[0:2 * NC, 0:HD], h2, w2v[:, :], start=True, stop=True).then_inc(pj_ready, 1)
                elif kind == "Sc":
                    pe.wait_ge(rope_done, ROPEN["nq", i] + 1)
                    pe.wait_ge(pj_dve, emptied("D", JOB["kc2", 0]))
                    for m in range(NT):
                        tok = slice(m * P, (m + 1) * P)
                        k = PLACE[4 + i] % 2
                        last = mm3(dst[:, 64 * m:64 * m + 64], qk_hi[:, k, 0, tok], qk_lo[:, k, 0, tok],
                                   kcb_hi[:, :], kcb_lo[:, :], True, True)
                    last.then_inc(pj_ready, 1)
                elif kind == "PcT":
                    pe.wait_ge(c_prob, i + 1)
                    for m in range(NT):
                        last = pe.transpose(dst[0:2 * NC, m * P:(m + 1) * P],
                                            pc[:, m, :, :].rearrange("p a n -> p (a n)"), ident)
                    last.then_inc(pj_ready, 1)
                elif kind == "gate":
                    pe.wait_ge(gate_sum, 2 * i + 2)
                    pe.wait_ge(fills_done, 7)
                    pe.wait_ge(rows_in, 16)
                    for g in range(2):
                        t = 2 * i + g
                        pe.matmul(dst[:, g * P:(g + 1) * P], ones[:, :], gsum[:, t % NSUM, :], start=True, stop=False)
                        r = R_ADA + 16 + t
                        pe.matmul(dst[:, g * P:(g + 1) * P], ident[0:R_END, r:r + 1].to_broadcast([R_END, P]), vecs[:, :],
                                  start=False, stop=True)
                        r = R_GPOST + t
                        last = pe.matmul(dst[:, (2 + g) * P:(3 + g) * P], ident[0:R_END, r:r + 1].to_broadcast([R_END, P]),
                                         vecs[:, :], start=True, stop=True)
                    last.then_inc(pj_ready, 1)

            def scores(s):
                p, a, b = INST[s]
                r = slice(HD * a, HD * a + HD)
                slot = PLACE[p] % 2
                if b is None:
                    pe.wait_ge(pj_dve, emptied("D", JOB["fk", p]))
                    k_hi, k_lo = qk_hi[r, slot, 1, :], qk_lo[r, slot, 1, :]
                else:
                    pe.wait_ge(rope_done, 1 + max(ROPEN["nq", p - 4], ROPEN["ks" if b == 0 else "kw", 0]))
                    k_hi, k_lo = nk_hi[r, b, :], nk_lo[r, b, :]
                if s == 0:
                    pe.wait_ge(consts_done, 3)
                    pe.wait_ge(ff_lo, 1)
                for k, (q, g, col, n) in enumerate(QT):
                    if col == 0 and s >= 1:
                        pe.wait_ge(exp_done, 3 * (s - 1) + g + 1)
                    dst = S_BANK[g]
                    tok = slice(q * P, (q + 1) * P)
                    mm3(dst[:, col:col + n], qk_hi[r, slot, 0, tok], qk_lo[r, slot, 0, tok], k_hi[:, 0:n], k_lo[:, 0:n],
                        True, False)
                    if b is None:
                        h = head_of(s)
                        pe.matmul(dst[:, col:col + n], sel_r[:, h:h + 1].to_broadcast([P, P]), cum_r[:, 0:n],
                                  start=False, stop=False)
                    last = pe.matmul(dst[:, col + n - P:col + n], ident_r[:, :], mask_r[:, :], start=False, stop=True)
                    if k != 1:
                        last.then_inc(s_ready, 1)

            def transposes(s, j):
                n = 3 * s + j
                if j == 0:
                    pe.wait_ge(p_ready, s + 1)
                if n >= 2:
                    pe.wait_ge(pt_lo_done, n - 1)
                for kt, col in PTG[j]:
                    for q in range(kt, NT):
                        o = POFF[q] + kt * P
                        last = pe.transpose(PT_BANK[n % 2][:, col + (q - kt) * P:col + (q - kt + 1) * P],
                                            prob[:, s % 2, o:o + P], ident)
                last.then_inc(pt_ready, 1)

            def values(s, j):
                p, a, b = INST[s]
                h = head_of(s)
                pe.wait_ge(pt_lo_done, 3 * s + j + 1)
                if b is None and j == 0:
                    pe.wait_ge(pj_dve, emptied("D", JOB["fv", 1 if p < 2 else 3]))
                if first_of_head(s) and j == 0 and s:
                    pe.wait_ge(y_done, heads_before(s))
                for kt, col in PTG[j]:
                    w = SEQ - kt * P
                    v = vf[:, kt, h, :, :] if b is None else vn[:, kt, 2 * b + a, :, :]
                    v = v.rearrange("p s d -> p (s d)")
                    pe.matmul(Y_BANK[:, kt * P:SEQ], v, pt_hi[:, j, col:col + w],
                              start=first_of_head(s) and j == 0, stop=False)
                    last = pe.matmul(Y_BANK[:, kt * P:SEQ], v, pt_lo[:, j, col:col + w], start=False,
                                     stop=b is None and j == 2)
                last.then_inc(pv_done, 1)
                if b is not None and last_of_head(s) and j == 2:
                    g = slice(NC * a, NC * a + NC)
                    pe.wait_ge(pj_dve, emptied("D", JOB["PcT", p - 4]))
                    v = vcb[g, :, :].rearrange("p s d -> p (s d)")
                    pe.matmul(Y_BANK[:, :], v, pcT[g, 0, :], start=False, stop=False)
                    pe.matmul(Y_BANK[:, :], v, pcT[g, 1, :], start=False, stop=True).then_inc(y_ready, 1)

            def project(kt, m, halves=(0, 1)):
                slot = SPLITN["wo", kt] % NSPLIT
                tok = slice(m * P, (m + 1) * P)
                pair = ORDER[kt]
                for half in halves:
                    w = slice(4 * half, 4 * half + 4)
                    last = mm3(bank[2 * m + half][:, :], hT_hi[:, pair, tok], hT_lo[:, pair, tok],
                               w_hi[:, slot, w, :], w_lo[:, slot, w, :], kt == 0, kt == KD - 1)
                    if kt == KD - 1:
                        last.then_inc(o_ready, 1)
                return last

            for j in PROLOGUE:
                if JOB[j] == EARLY_X_AT:
                    pe.wait_ge(kon_in, 16)
                    pe.wait_ge(xn_done, NT)
                    for d in range(EARLY_X):
                        x_transposes(d, bank[d]).then_inc(xT_ready, 1)
                job(j)
            for s in range(NI + 1):
                if 1 <= s <= NI:
                    transposes(s - 1, 0)
                    transposes(s - 1, 1)
                if s < NI:
                    scores(s)
                if 1 <= s <= NI:
                    transposes(s - 1, 2)
                for j in FILL[s] if s < NI else []:
                    job(j)
                for kt, m in EARLY_OUT.get(s, ()):
                    wait_split(("wo", kt))
                    pe.wait_ge(yl_done, kt + 1)
                    if (kt, m) == (0, 3):
                        pe.wait_ge(pj_act, emptied("A", len(JOBS) - 1))
                        pe.wait_ge(pj_dve, emptied("D", len(JOBS) - 1))
                    if (kt, m) == (0, 0):
                        pe.wait_ge(exp_done, 3 * NI)
                    project(kt, m)
                if 1 <= s <= NI:
                    for g in range(3):
                        values(s - 1, g)

            for kt, m in LATER_OUT:
                if (kt, m) == (0, 1):
                    pe.wait_ge(pt_lo_done, 3 * NI)
                    pe.wait_ge(y_done, FOX_H + NSA_H)
                last = project(kt, m)
                if m == 2:
                    last.then_inc(wo_used, 1)
            for m in range(NT):
                for halves in [(0, 1)] if m < NT - 1 else [(0,), (1,)]:
                    for kt in range(KD // 2, KD):
                        if m == 0:
                            wait_split(("wo", kt))
                            pe.wait_ge(yl_done, kt + 1)
                        project(kt, m, halves)


_INS = ["x", "w_ada", "w_in", "b_forget", "w_cmp_k1", "w_cmp_k2", "w_cmp_v1", "w_cmp_v2", "w_out"]
_VECTORS = ["c", "g_pre", "b_ada", "g_post", "pe_cmp_k", "pe_cmp_v"]
_STACKED = ("w_ada", "w_in", "w_cmp_k1", "w_cmp_k2", "w_cmp_v1", "w_cmp_v2", "w_out")


def _rope_tables():
    import numpy as np
    inv = (1.0 / (np.float32(10000.0) ** (np.arange(0, HD, 2, dtype=np.float32) / np.float32(HD)))).astype(np.float32)
    ang = np.arange(SEQ, dtype=np.float32)[:, None] * inv[None, :]
    cos, sin = np.cos(ang).T, np.sin(ang).T
    return np.ascontiguousarray(np.stack([np.tile(cos, (4, 1)), np.concatenate([-sin, sin, -sin, sin])], 1).astype(np.float32))


def _constants():
    import numpy as np
    k = np.zeros((P, K_END), np.float32)
    k[:, K_ID:K_ID + P] = np.eye(P)
    row = np.arange(P)
    k[:, K_MASK:K_MASK + P] = np.where(row[None, :] <= row[:, None], 0.0, NEG)
    n = np.arange(NC)
    for m in range(NT):
        seen = (n[None, :] * CMP_STRIDE + CMP_BLOCK - 1 <= m * P + row[:, None]) & (n[None, :] < NCMP)
        k[:, K_CMASK + m * NC:K_CMASK + (m + 1) * NC] = np.where(seen, 0.0, NEG)
    for h in range(8):
        k[h, K_SEL + h] = k[32 + h, K_SEL + h] = 1.0
    return k


def kernel(**inputs):
    import numpy as _np
    import concourse.bacc as _bacc
    from concourse import mybir as _mybir
    from concourse.bass_utils import run_bass_kernel_spmd as _run

    nc = _bacc.Bacc("TRN2", target_bir_lowering=False, num_devices=1)
    given = {}
    for name in _INS:
        a = _np.ascontiguousarray(inputs[name])
        given[name] = a[0] if name in _STACKED or name == "x" else a
    rows = _np.concatenate([_np.asarray(inputs[name]).reshape(-1, P) for name in _VECTORS])
    given["vec_rows"], given["vec_cols"] = rows, _np.ascontiguousarray(rows.T)
    given["rope"], given["consts"] = _rope_tables(), _constants()
    arrays, args = {}, []
    for name, a in given.items():
        arrays[f"in_{name}_dram"] = a
        args.append(nc.dram_tensor(f"in_{name}_dram", a.shape, _mybir.dt.from_np(a.dtype), kind="ExternalInput").ap())
    args.append(nc.dram_tensor("out_0_dram", (SEQ, DM), _mybir.dt.float32, kind="ExternalOutput").ap())
    hybrid_layer_kernel(nc, *args)
    r = _run(nc, [arrays], core_ids=[0])
    return r.results[0]["out_0_dram"].reshape(1, SEQ, DM)
```
